# Optimizing a Trainium2 kernel written in Bass

```python
import math
import jax, jax.numpy as jnp
from jax import lax
import numpy as np

D_MODEL = 1024
BATCH = 1
SEQ = 512
DEPTH = 1

N_FOURIER_GROUPS = 4
FOURIER_GROUP_DIM = 128
FOURIER_WIDTH = N_FOURIER_GROUPS * FOURIER_GROUP_DIM
DIL_PATTERNS = ((128, 1), (512, 4), (2048, 16))
N_DIL_GROUPS = 3
HEADS_PER_DIL_GROUP = 4
DIL_HEAD_DIM = 64
DIL_HEADS = N_DIL_GROUPS * HEADS_PER_DIL_GROUP
DIL_WIDTH = DIL_HEADS * DIL_HEAD_DIM
DIL_OUT_WIDTH = HEADS_PER_DIL_GROUP * DIL_HEAD_DIM
MEM_LEN = 256
MEM_HEADS = 4
MEM_HEAD_DIM = 128
MEM_WIDTH = MEM_HEADS * MEM_HEAD_DIM
N_BRANCHES = 3
COL_A_END = FOURIER_WIDTH
COL_B_END = COL_A_END + 3 * DIL_WIDTH
COL_C_END = COL_B_END + MEM_WIDTH
COL_TOTAL = COL_C_END + N_BRANCHES * D_MODEL
REL_BUCKETS = 32
REL_MAX_DIST = 1024
PEER_HEADS = 8
PEER_KEYS = 128
PEER_EXPERTS = PEER_KEYS * PEER_KEYS
PEER_QUERY_DIM = 128
PEER_HALF = PEER_QUERY_DIM // 2
PEER_TOPK = 16
PEER_CHUNK = 128
ALPHA = (2.0 * DEPTH) ** 0.25
BETA = (8.0 * DEPTH) ** -0.25
LN_EPS = 1e-5
NEG_INF = -1e30

kernel_name = "hybrid_fnet_dilated_memattn_peer_deepnorm"

def layer_norm(x, g, b):
    xf = x.astype(jnp.float32)
    mu = jnp.mean(xf, -1, keepdims=True)
    var = jnp.mean(jnp.square(xf - mu), -1, keepdims=True)
    y = (xf - mu) * lax.rsqrt(var + LN_EPS) * g.astype(jnp.float32) + b.astype(jnp.float32)
    return y.astype(x.dtype)

def t5_bucket(rel):
    half = REL_BUCKETS // 2
    max_exact = half // 2
    ret = jnp.where(rel > 0, half, 0)
    n = jnp.abs(rel)
    nf = jnp.maximum(n, 1).astype(jnp.float32)
    large = max_exact + (jnp.log(nf / max_exact) / math.log(REL_MAX_DIST / max_exact)
                         * (half - max_exact)).astype(jnp.int32)
    large = jnp.minimum(large, half - 1)
    return ret + jnp.where(n < max_exact, n, large)

def fourier_mix(u):
    f = jnp.fft.fftn(u.astype(jnp.float32), axes=(1, 3), norm="ortho")
    return jnp.real(f).astype(u.dtype)

def dilated_window_attention(q, k, v, bias_table, window, dilation):
    bsz, seq, heads, hd = q.shape
    steps = window // (2 * dilation)
    blk = steps
    sub_len = seq // dilation
    n_blk = -(-sub_len // blk)
    pad_len = n_blk * blk

    def sub(t):
        return t.reshape(bsz, sub_len, dilation, heads, hd)

    qs = jnp.pad(sub(q), ((0, 0), (0, pad_len - sub_len), (0, 0), (0, 0), (0, 0)))
    qs = qs.reshape(bsz, n_blk, blk, dilation, heads, hd)

    def windows(t):
        tp = jnp.pad(sub(t), ((0, 0), (blk, pad_len - sub_len + blk), (0, 0), (0, 0), (0, 0)))
        tp = tp.reshape(bsz, n_blk + 2, blk, dilation, heads, hd)
        return jnp.concatenate([tp[:, :-2], tp[:, 1:-1], tp[:, 2:]], axis=2)

    kw, vw = windows(k), windows(v)
    s = jnp.einsum('bnqrhc,bnkrhc->bnrhqk', qs, kw,
                   preferred_element_type=jnp.float32) * (hd ** -0.5)
    step_off = jnp.arange(3 * blk)[None, :] - blk - jnp.arange(blk)[:, None]
    band = jnp.abs(step_off) <= steps
    key_step = jnp.arange(n_blk)[:, None] * blk + jnp.arange(3 * blk)[None, :] - blk
    inside = (key_step >= 0) & (key_step < sub_len)
    mask = band[None] & inside[:, None, :]
    bias = jnp.transpose(bias_table[t5_bucket(step_off * dilation)], (2, 0, 1)).astype(jnp.float32)
    s = jnp.where(mask[None, :, None, None], s + bias[None, None, None], NEG_INF)
    m = jnp.max(s, -1, keepdims=True)
    p = jnp.exp(s - m)
    den = jnp.sum(p, -1)
    o = jnp.einsum('bnrhqk,bnkrhc->bnqrhc', p, vw.astype(jnp.float32))
    o = o / jnp.transpose(den, (0, 1, 4, 2, 3))[..., None]
    lse = jnp.transpose(m[..., 0] + jnp.log(den), (0, 1, 4, 2, 3))
    o = o.reshape(bsz, pad_len, dilation, heads, hd)[:, :sub_len].reshape(bsz, seq, heads, hd)
    lse = lse.reshape(bsz, pad_len, dilation, heads)[:, :sub_len].reshape(bsz, seq, heads)
    return o, lse

def mixing_sublayer(h, mem, rel_bias, w_in, b_in, w_a, w_b, w_c, w_mem_kv, w_o, ln_g, ln_b):
    bsz, seq, d = h.shape
    z = h @ w_in + b_in
    za = z[..., :COL_A_END].reshape(bsz, seq, N_FOURIER_GROUPS, FOURIER_GROUP_DIM)
    y_a = fourier_mix(za).reshape(bsz, seq, FOURIER_WIDTH) @ w_a
    qkv = z[..., COL_A_END:COL_B_END].reshape(bsz, seq, 3, N_DIL_GROUPS, HEADS_PER_DIL_GROUP, DIL_HEAD_DIM)
    outs, lses = [], []
    for g, (win, dil) in enumerate(DIL_PATTERNS):
        o, lse = dilated_window_attention(
            qkv[:, :, 0, g], qkv[:, :, 1, g], qkv[:, :, 2, g],
            rel_bias[:, g * HEADS_PER_DIL_GROUP:(g + 1) * HEADS_PER_DIL_GROUP], win, dil)
        outs.append(o)
        lses.append(lse)
    wts = jax.nn.softmax(jnp.stack(lses), axis=0)
    o_b = jnp.einsum('gbsh,gbshc->bshc', wts, jnp.stack(outs)).astype(h.dtype)
    y_b = o_b.reshape(bsz, seq, DIL_OUT_WIDTH) @ w_b
    q_c = z[..., COL_B_END:COL_C_END].reshape(bsz, seq, MEM_HEADS, MEM_HEAD_DIM)
    kv = (mem @ w_mem_kv).reshape(bsz, mem.shape[1], 2, MEM_HEADS, MEM_HEAD_DIM)
    sc = jnp.einsum('bshc,bmhc->bhsm', q_c, kv[:, :, 0],
                    preferred_element_type=jnp.float32) * (MEM_HEAD_DIM ** -0.5)
    pc = jax.nn.softmax(sc, axis=-1).astype(h.dtype)
    y_c = jnp.einsum('bhsm,bmhc->bshc', pc, kv[:, :, 1]).reshape(bsz, seq, MEM_WIDTH) @ w_c
    gates = jax.nn.sigmoid(z[..., COL_C_END:].reshape(bsz, seq, N_BRANCHES, d))
    merged = gates[:, :, 0] * y_a + gates[:, :, 1] * y_b + gates[:, :, 2] * y_c
    return layer_norm(ALPHA * h + merged @ w_o, ln_g, ln_b)

def peer_sublayer(h, w_pq, sub_keys1, sub_keys2, u_tab, v_tab, ln_g, ln_b):
    bsz, seq, d = h.shape
    n_tok = bsz * seq
    xt = h.reshape(n_tok, d)
    q = (xt @ w_pq).reshape(n_tok, PEER_HEADS, 2, PEER_HALF).astype(jnp.float32)
    s1 = jnp.einsum('thc,kc->thk', q[:, :, 0], sub_keys1.astype(jnp.float32))
    s2 = jnp.einsum('thc,kc->thk', q[:, :, 1], sub_keys2.astype(jnp.float32))
    v1, i1 = lax.top_k(s1, PEER_TOPK)
    v2, i2 = lax.top_k(s2, PEER_TOPK)
    cand = (v1[..., :, None] + v2[..., None, :]).reshape(n_tok, PEER_HEADS, PEER_TOPK * PEER_TOPK)
    sc, ic = lax.top_k(cand, PEER_TOPK)
    e1 = jnp.take_along_axis(i1, ic // PEER_TOPK, axis=-1)
    e2 = jnp.take_along_axis(i2, ic % PEER_TOPK, axis=-1)
    experts = (e1 * PEER_KEYS + e2).reshape(n_tok, PEER_HEADS * PEER_TOPK)
    gate = jax.nn.softmax(sc, axis=-1).reshape(n_tok, PEER_HEADS * PEER_TOPK).astype(h.dtype)
    n_chunks = n_tok // PEER_CHUNK

    def chunk_fn(args):
        xc, ec, gc = args
        act = jax.nn.gelu(jnp.einsum('tkd,td->tk', u_tab[ec], xc), approximate=False)
        return jnp.einsum('tk,tkd->td', gc * act, v_tab[ec])

    y = lax.map(chunk_fn, (xt.reshape(n_chunks, PEER_CHUNK, d),
                           experts.reshape(n_chunks, PEER_CHUNK, -1),
                           gate.reshape(n_chunks, PEER_CHUNK, -1)))
    y = y.reshape(bsz, seq, d)
    return layer_norm(ALPHA * h + y, ln_g, ln_b)

def setup_inputs(seed: int = 0) -> dict:
    key = jax.random.key(seed)
    ks = jax.random.split(key, 24)
    f32 = jnp.float32

    def nrm(k, shape, scale):
        return jax.random.normal(k, shape, f32) * scale

    return {
        "x": nrm(ks[0], (BATCH, SEQ, D_MODEL), 1.0),
        "mem": nrm(ks[1], (BATCH, MEM_LEN, D_MODEL), 1.0),
        "rel_bias": nrm(ks[2], (REL_BUCKETS, DIL_HEADS), 0.5),
        "ln0_g": 1.0 + nrm(ks[3], (D_MODEL,), 0.02),
        "ln0_b": nrm(ks[4], (D_MODEL,), 0.02),
        "w_in": nrm(ks[5], (DEPTH, D_MODEL, COL_TOTAL), D_MODEL ** -0.5),
        "b_in": nrm(ks[6], (DEPTH, COL_TOTAL), 0.02),
        "w_a": nrm(ks[7], (DEPTH, FOURIER_WIDTH, D_MODEL), FOURIER_WIDTH ** -0.5),
        "w_b": nrm(ks[8], (DEPTH, DIL_OUT_WIDTH, D_MODEL), DIL_OUT_WIDTH ** -0.5),
        "w_c": nrm(ks[9], (DEPTH, MEM_WIDTH, D_MODEL), MEM_WIDTH ** -0.5),
        "w_mem_kv": nrm(ks[10], (DEPTH, D_MODEL, 2 * MEM_WIDTH), D_MODEL ** -0.5),
        "w_o": nrm(ks[11], (DEPTH, D_MODEL, D_MODEL), BETA * D_MODEL ** -0.5),
        "ln1_g": 1.0 + nrm(ks[12], (DEPTH, D_MODEL), 0.02),
        "ln1_b": nrm(ks[13], (DEPTH, D_MODEL), 0.02),
        "w_pq": nrm(ks[14], (DEPTH, D_MODEL, PEER_HEADS * PEER_QUERY_DIM), D_MODEL ** -0.5),
        "sub_keys1": nrm(ks[15], (DEPTH, PEER_KEYS, PEER_HALF), PEER_HALF ** -0.5),
        "sub_keys2": nrm(ks[16], (DEPTH, PEER_KEYS, PEER_HALF), PEER_HALF ** -0.5),
        "u_tab": nrm(ks[17], (DEPTH, PEER_EXPERTS, D_MODEL), D_MODEL ** -0.5),
        "v_tab": nrm(ks[18], (DEPTH, PEER_EXPERTS, D_MODEL), BETA),
        "ln2_g": 1.0 + nrm(ks[19], (DEPTH, D_MODEL), 0.02),
        "ln2_b": nrm(ks[20], (DEPTH, D_MODEL), 0.02),
    }

def reference(x, mem, rel_bias, ln0_g, ln0_b, w_in, b_in, w_a, w_b, w_c, w_mem_kv, w_o,
              ln1_g, ln1_b, w_pq, sub_keys1, sub_keys2, u_tab, v_tab, ln2_g, ln2_b):
    h = layer_norm(x, ln0_g, ln0_b)
    for l in range(DEPTH):
        h = mixing_sublayer(h, mem, rel_bias, w_in[l], b_in[l], w_a[l], w_b[l], w_c[l],
                            w_mem_kv[l], w_o[l], ln1_g[l], ln1_b[l])
        h = peer_sublayer(h, w_pq[l], sub_keys1[l], sub_keys2[l], u_tab[l], v_tab[l],
                          ln2_g[l], ln2_b[l])
    return h


_drawn_inputs = setup_inputs


def setup_inputs(seed=0):
    import zlib

    import numpy as np

    out = dict(_drawn_inputs(seed))
    spreads = {}
    factors = {'b_in': 3.191, 'ln2_g': 2.836, 'ln2_b': 2.949}
    for name, (base, spread) in spreads.items():
        noise = np.random.default_rng([zlib.crc32(name.encode()), seed]).standard_normal(out[name].shape)
        drawn = base * np.exp(spread * noise) if base else spread * noise
        out[name] = __import__('jax').numpy.asarray(drawn.astype(out[name].dtype))
    for name, factor in factors.items():
        out[name] = (out[name] * factor).astype(out[name].dtype)
    return out
```

```python
from contextlib import ExitStack
import math

import numpy as np

import concourse.bass as bass
from concourse import mybir

F32 = mybir.dt.float32
U32 = mybir.dt.uint32
I32 = mybir.dt.int32
ALU = mybir.AluOpType
ACT = mybir.ActivationFunctionType
AX = mybir.AxisListType

P = 128
D = 1024
SEQ = 512
TILES = SEQ // P
DK = D // P
MEM = 256
CHUNK = 256
RING = 4
BANKS = 8
BUCKETS = 32
DIL_HEADS = 4
HD = 64
DELTAS = 2 * P
TABLES = 2 * TILES - 1 + 2
ALPHA = 2.0 ** 0.25
EPS = 1e-5
RSQRT_GUESS = float(0x5F3759DF)
SCALE_B = HD ** -0.5
SCALE_C = 128 ** -0.5

ZA, QK, VV, QC, GA = range(0, 2), range(2, 8), range(8, 11), range(11, 13), range(13, 25)


HEADS = 8
TOPK = 16
KEYS = 128
STEPS = TILES * HEADS
LOWEST = -3.0e38


class Units:

    def __init__(self):
        self.index, self.bank, self.reader, self.ordinal, self.before = {}, {}, {}, {}, {}
        self.emptied = {"act": 0, "dve": 0}
        self.owner = [None] * BANKS
        self.turn = 0

    def add(self, key, reader, bank=None, width=1):
        if bank is None:
            bank, self.turn = self.turn, (self.turn + 1) % BANKS
        self.before[key] = {self.owner[b] for b in range(bank, bank + width)} - {None}
        for b in range(bank, bank + width):
            self.owner[b] = key
        self.index[key], self.bank[key], self.reader[key] = len(self.index), bank, reader
        self.emptied[reader] += 1
        self.ordinal[key] = self.emptied[reader]


def plan():
    u = Units()
    for m in range(2):
        for q in range(2):
            u.add(("memT", m, q), "act")
    for n in range(4):
        u.add(("kT", n), "act")
    for c in range(2):
        for m in range(2):
            u.add(("vm", c, m), "act")
    u.add(("bT",), "act")
    u.add(("KK",), "dve")
    for b in range(6):
        u.add(("beta", b), "dve")
    for r in range(TILES):
        for q in range(2):
            u.add(("h0T", r, q), "act")
    for n in range(4):
        u.add(("z", n), "act")
    for r in range(TILES):
        for g in range(2):
            u.add(("PQ", r, g), "dve")
    for g in range(4):
        u.add(("Y", g), "act")
    for n in range(4, 16):
        u.add(("z", n), "act")
    for c in range(3):
        for r in range(TILES):
            u.add(("v", c, r), "dve")
    for n in range(22, 26):
        u.add(("z", n), "act")
    N = TILES * DIL_HEADS
    def S(i): u.add(("S", i), "act", bank=2 * (i % 2), width=2)
    S(0)
    for i in range(N + 1):
        if i + 1 < N:
            S(i + 1)
        if i >= 1:
            u.add(("O", i - 1), "dve", bank=6 + i % 2)
        if i < N:
            u.add(("T0", i), "act", bank=4)
            u.add(("T1", i), "dve", bank=5)
    u.turn = 0
    for j in range(DK):
        for b in range(3):
            u.add(("G", j, b), "act")
        for b in range(3):
            u.add(("Yo", j, b), "dve")
    for c in range(4):
        for r in range(TILES):
            u.add(("WO", c, r), "dve")
    for r in range(TILES):
        for q in range(2):
            u.add(("h1T", r, q), "act")
    for n in range(8):
        u.add(("Q", n), "act")
        if n >= 1:
            for q in range(2):
                u.add(("SC", n - 1, q), "dve")
    for q in range(2):
        u.add(("SC", 7, q), "dve")
    return u


def chunk_plan():
    c = []
    for n in range(4):
        c.append((("kv", n), ("kT", 2 * n + 1) if n < 2 else ("vm", n - 2, 1)))
    for n in list(ZA) + list(QK):
        c.append((("in", n), ("z", 2 * n + 1)))
    for n in VV:
        c.append((("in", n), ("v", n - VV[0], TILES - 1)))
    for n in QC:
        c.append((("in", n), ("z", 2 * n + 1)))
    for jj in range(4):
        for b in range(3):
            c.append((("in", GA[0] + 4 * b + jj), ("G", 2 * jj + 1, b)))
        c.append((("wy", jj), ("Yo", 2 * jj + 1, 2)))
    for n in range(4):
        c.append((("o", n), ("WO", n, TILES - 1)))
    for n in range(4):
        c.append((("pq", n), ("Q", 2 * n + 1)))
    return c


def build(nc, x, mem, rel_bias, ln0_g, ln0_b, w_in, b_in, w_a, w_b, w_c, w_mem_kv, w_o,
          ln1_g, ln1_b, w_pq, sub_keys1, sub_keys2, u_tab, v_tab, ln2_g, ln2_b,
          c_onehot, c_mask, c_chan, c_cos, c_sin, out):
    beta_dram = nc.dram_tensor("beta_rows", [DIL_HEADS, TABLES, DELTAS], F32).ap()
    rows = lambda t: t[0].rearrange("(m r) d -> r m d", r=TILES)
    x_rows, out_rows = rows(x), rows(out)
    with ExitStack() as outer:
        def keep(name, shape, dt=F32):
            return outer.enter_context(nc.sbuf_tensor(name, shape, dt))

        fh = keep("fh", [P, 12288])
        ident = keep("ident", [P, P])
        scores = fh[:, 0:8192].rearrange("p (s k) -> p s k", s=32)
        h1 = fh[:, 8192:12288].rearrange("p (r d) -> p r d", r=TILES)
        with ExitStack() as ctx:
            mixing(nc, ctx, fh, ident, scores, h1, x_rows, mem, rel_bias, ln0_g, ln0_b, w_in, b_in, w_a, w_b, w_c,
                   w_mem_kv, w_o, ln1_g, ln1_b, w_pq, sub_keys1, sub_keys2,
                   c_onehot, c_mask, c_chan, c_cos, c_sin, beta_dram)
        build_peer(nc, h1, scores, u_tab[0], v_tab[0], ident, ln2_g, ln2_b, out_rows)


def mixing(nc, ctx, fh, ident, scores, h1, x_rows, mem, rel_bias, ln0_g, ln0_b, w_in, b_in, w_a, w_b, w_c,
           w_mem_kv, w_o, ln1_g, ln1_b, w_pq, sub_keys1, sub_keys2,
           c_onehot, c_mask, c_chan, c_cos, c_sin, beta_dram):
    def sb(name, shape, dt=F32):
        return ctx.enter_context(nc.sbuf_tensor(name, shape, dt))

    def sem(name):
        return ctx.enter_context(nc.semaphore(name))

    units, chunks = plan(), chunk_plan()
    N = TILES * DIL_HEADS

    h0 = sb("h0", [P, TILES, D])
    hT = sb("hT", [P, DK, SEQ])
    zT = sb("zT", [P, 16, SEQ])
    v_sb = sb("v_sb", [P, TILES, 3 * DIL_HEADS * HD])
    ring = sb("ring", [P, RING, 8, CHUNK])
    oA = sb("oA", [P, 4, SEQ])
    oBC = sb("oBC", [P, 6, SEQ])
    oB, oC = oBC[:, 0:2, :], oBC[:, 2:6, :]
    kT = sb("kT", [P, 4, MEM])
    vm = sb("vm", [P, 2, 512])
    gains = sb("gains", [P, 2, D])
    v_bias = sb("v_bias", [P, 768])
    bT = sb("bT", [P, 50])
    b_rows = sb("b_rows", [50, P])
    chan = sb("chan", [P, 2 * P])
    flip = sb("flip", [P, P])
    keys = sb("keys", [P, P])
    KK = sb("KK", [P, 2 * P])
    relb = sb("relb", [BUCKETS, 3 * DIL_HEADS])
    stats = sb("stats", [P, TILES, 2, 6])
    moments = sb("moments", [P, TILES, 2])
    rs = sb("rs", [P, 5, TILES])
    mx = sb("mx", [P, 2, 2])
    nm = sb("nm", [P, 2, 2])
    sums = sb("sums", [P, 2, 2])
    rinv = sb("rinv", [P, 2, 2])
    ps = ctx.enter_context(nc.psum_tensor("ps", [P, BANKS, 512], F32))

    zaT = fh[:, 0:2048].rearrange("p (g s) -> p g s", g=4)
    pq = fh[:, 2048:6144].rearrange("p (r g c) -> p r g c", r=TILES, g=4)
    cos_t = fh[:, 6144:8192].rearrange("p (r s) -> p r s", r=TILES)
    sin_t = fh[:, 8192:10240].rearrange("p (r s) -> p r s", r=TILES)
    mem_sb = fh[:, 10240:12288].rearrange("p (m d) -> p m d", m=2)
    memT = zT[:, 8:12, :].rearrange("p a (b m) -> p (a b) m", m=MEM)
    onehot = zT[0:BUCKETS, 0:5, :].rearrange("p a b -> p (a b)")[:, 0:TABLES * DELTAS]
    mask = zT[0:DIL_HEADS, 12:16, :].rearrange("p a b -> p (a b)")
    beta = oBC[0:DIL_HEADS, :, :].rearrange("p a b -> p (a b)")[:, 0:TABLES * DELTAS]
    mask2 = hT[0:DIL_HEADS, 0:5, :].rearrange("p a b -> p (a b)")[:, 0:TABLES * DELTAS]
    bias = fh[:, 0:DIL_HEADS * TABLES * P].rearrange("p (h j m) -> p h j m", h=DIL_HEADS, j=TABLES)
    B0 = DIL_HEADS * TABLES * P
    prob = fh[:, B0:B0 + 2048].rearrange("p (b k) -> p b k", b=2)
    probT = fh[:, B0 + 2048:B0 + 4096].rearrange("p (b j q) -> p b j q", b=2, j=8)
    wb = fh[:, B0 + 4096:B0 + 6144].rearrange("p (k n) -> p k n", k=2)
    merged = zT[:, 0:8, :]
    sig = zT[:, 8:11, :]
    part = zT[:, 11:13, :]
    qT = zT[:, 13:15, :]

    x_in, mem_in, small_in, gain_in = sem("x_in"), sem("mem_in"), sem("small_in"), sem("gain_in")
    onehot_in, fourier_in, wb_in = sem("onehot_in"), sem("fourier_in"), sem("wb_in")
    mask_in = sem("mask_in")
    beta_out, bias_in = sem("beta_out"), sem("bias_in")
    ring_in = [sem(f"ring_in{j}") for j in range(RING)]
    full = sem("psum_full")
    emptied = {"act": sem("act_emptied"), "dve": sem("dve_emptied")}
    consts = sem("consts")
    h0_ready, h1_ready = sem("h0_ready"), sem("h1_ready")
    nm_ready, exp_ready, prob_ready = sem("nm_ready"), sem("exp_ready"), sem("prob_ready")
    dve_step = sem("mix_dve_step")
    sig_ready = sem("sig_ready")

    def bank(key, lo=0, hi=512):
        return ps[:, units.bank[key], lo:hi]

    def wait_full(eng, key):
        eng.wait_ge(full, units.index[key] + 1)

    def wait_done(eng, key):
        eng.wait_ge(emptied[units.reader[key]], units.ordinal[key])

    chunk_at = {key: i for i, (key, _) in enumerate(chunks)}

    block = ctx.enter_context(nc.Block())

    @block.sync
    def _(sp):
        sp.dma_start(mem_sb, mem[0].rearrange("(m p) d -> p m d", p=P)).then_inc(mem_in, 16)

        def load(i):
            (what, n), _ = chunks[i]
            if i >= RING:
                sp.wait_ge(full, units.index[chunks[i - RING][1]] + 1)
            if what == "wy":
                for w, lo in ((w_a, 0), (w_c, 4)):
                    sp.dma_start(ring[:, i % RING, lo:lo + 4, :],
                                 w[0].rearrange("(k p) n -> p k n", p=P)[:, :, n * CHUNK:(n + 1) * CHUNK],
                                 ).then_inc(ring_in[i % RING], 16)
            else:
                w = {"kv": w_mem_kv, "in": w_in, "o": w_o, "pq": w_pq}[what]
                sp.dma_start(ring[:, i % RING, :, :],
                             w[0].rearrange("(k p) n -> p k n", p=P)[:, :, n * CHUNK:(n + 1) * CHUNK],
                             ).then_inc(ring_in[i % RING], 16)

        load(0)
        for r in range(TILES):
            sp.dma_start(h0[:, r, :], x_rows[r]).then_inc(x_in, 16)
        for i in range(1, 4):
            load(i)
        for i in range(4, len(chunks)):
            if i == 6:
                sp.wait_ge(full, units.index[("memT", 1, 1)] + 1)
            load(i)
            if i == 10:
                wait_full(sp, ("Y", 3))
                sp.wait_ge(beta_out, 16)
                sp.dma_start(bias.rearrange("p h j m -> p (h j) m"),
                             bass.AP(tensor=beta_dram.tensor, offset=0,
                                     ap=[[1, P], [DELTAS, DIL_HEADS * TABLES], [1, P]])).then_inc(bias_in, 16)
                sp.dma_start(wb, w_b[0].rearrange("(k p) n -> p k n", p=P)).then_inc(wb_in, 16)

    @block.gpsimd
    def _(pool):
        row = lambda a: a.rearrange("(a n) -> a n", a=1)
        pool.dma_start(b_rows[:], b_in[0].rearrange("(t p) -> t p", p=P)).then_inc(small_in, 16)
        pool.dma_start(keys[:, 0:HD], sub_keys1[0]).then_inc(small_in, 16)
        pool.dma_start(keys[:, HD:2 * HD], sub_keys2[0]).then_inc(small_in, 16)
        pool.dma_start(relb[:], rel_bias).then_inc(small_in, 16)
        pool.dma_start(onehot, c_onehot).then_inc(onehot_in, 16)
        pool.dma_start(mask2, c_mask).then_inc(mask_in, 16)
        pool.dma_start(gains[:, 0, :], row(ln0_g).broadcast_to([P, D])).then_inc(gain_in, 16)
        pool.dma_start(gains[:, 1, :], row(ln0_b).broadcast_to([P, D])).then_inc(gain_in, 16)
        nc.gpsimd.memset(ident[:], 0.0).then_inc(consts, 1)
        nc.gpsimd.memset(flip[:], 0.0).then_inc(consts, 1)
        nc.gpsimd.memset(KK[:], 0.0).then_inc(consts, 1)
        pool.wait_ge(consts, 3)
        nc.gpsimd.affine_select(out=ident[:], in_=ident[:], compare_op=ALU.not_equal, fill=1.0,
                                base=0, pattern=[[-1, P]], channel_multiplier=1).then_inc(consts, 1)
        nc.gpsimd.affine_select(out=flip[:], in_=flip[:], compare_op=ALU.not_equal, fill=1.0,
                                base=1 - P, pattern=[[1, P]], channel_multiplier=1).then_inc(consts, 1)
        pool.dma_start(chan[:], c_chan).then_inc(fourier_in, 16)
        pool.dma_start(v_bias[:], row(b_in[0, 2048:2816]).broadcast_to([P, 768])).then_inc(fourier_in, 16)
        pool.dma_start(cos_t, c_cos.rearrange("(r p) s -> p r s", p=P)).then_inc(fourier_in, 16)
        pool.dma_start(sin_t, c_sin.rearrange("(r p) s -> p r s", p=P)).then_inc(fourier_in, 16)
        for b in range(6):
            wait_done(pool, ("beta", b))
        pool.dma_start(beta_dram.rearrange("h j m -> h (j m)"), beta).then_inc(beta_out, 16)
        pool.wait_ge(h0_ready, TILES)
        pool.dma_start(gains[:, 0, :], row(ln1_g[0]).broadcast_to([P, D])).then_inc(gain_in, 16)
        pool.dma_start(gains[:, 1, :], row(ln1_b[0]).broadcast_to([P, D])).then_inc(gain_in, 16)

    @block.tensor
    def _(pe):
        def begin(key):
            for k in sorted(units.before[key], key=lambda k: units.index[k]):
                wait_done(pe, k)

        def chunk(key):
            i = chunk_at[key]
            n = sum(2 if chunks[j][0][0] == "wy" else 1 for j in range(i % RING, i + 1, RING))
            pe.wait_ge(ring_in[i % RING], 16 * n)
            return ring[:, i % RING, :, :]

        def mm(o, lhsT, rhs, start, stop):
            return nc.tensor.matmul(o, lhsT, rhs, start=start, stop=stop, skip_group_check=True)

        def end(ins):
            ins.then_inc(full, 1)

        pe.wait_ge(consts, 5)
        pe.wait_ge(mem_in, 16)
        for m in range(2):
            for q in range(2):
                key = ("memT", m, q)
                begin(key)
                for k in range(4):
                    d = 4 * q + k
                    last = nc.tensor.transpose(bank(key, k * P, (k + 1) * P), mem_sb[:, m, d * P:(d + 1) * P], ident[:])
                end(last)
        for m in range(2):
            for q in range(2):
                wait_done(pe, ("memT", m, q))
        for n in range(4):
            w = chunk(("kv", n // 2))
            key = ("kT", n)
            begin(key)
            for k in range(DK):
                last = mm(bank(key, 0, MEM), w[:, k, (n % 2) * P:(n % 2 + 1) * P], memT[:, k, :], k == 0, k == DK - 1)
            end(last)
        for c in range(2):
            w = chunk(("kv", 2 + c))
            for m in range(2):
                key = ("vm", c, m)
                begin(key)
                for k in range(DK):
                    last = mm(bank(key, 0, CHUNK), memT[:, k, m * P:(m + 1) * P], w[:, k, :], k == 0, k == DK - 1)
                end(last)
        pe.wait_ge(small_in, 64)
        begin(("bT",))
        end(nc.tensor.transpose(bank(("bT",), 0, 50), b_rows[:], ident[0:50, 0:50]))
        begin(("KK",))
        end(nc.tensor.transpose(bank(("KK",), 0, P), keys[:], ident[:]))
        pe.wait_ge(onehot_in, 16)
        cuts = [0, 512, 1024, 1536, 1792, 2048, 2304]
        for b in range(6):
            g = (0, 0, 0, 0, 1, 2)[b]
            key = ("beta", b)
            begin(key)
            end(mm(ps[0:DIL_HEADS, units.bank[key], 0:cuts[b + 1] - cuts[b]],
                   relb[:, DIL_HEADS * g:DIL_HEADS * (g + 1)], onehot[:, cuts[b]:cuts[b + 1]], True, True))

        def transposed(name, src, ready):
            for r in range(TILES):
                pe.wait_ge(ready, r + 1)
                for q in range(2):
                    key = (name, r, q)
                    begin(key)
                    for k in range(4):
                        d = 4 * q + k
                        last = nc.tensor.transpose(bank(key, k * P, (k + 1) * P), src[:, r, d * P:(d + 1) * P], ident[:])
                    end(last)
            for r in range(TILES):
                for q in range(2):
                    wait_done(pe, (name, r, q))

        def project(n):
            w = chunk(("in", n // 2))
            key = ("z", n)
            begin(key)
            for k in range(DK):
                last = mm(bank(key), w[:, k, (n % 2) * P:(n % 2 + 1) * P], hT[:, k, :], k == 0, k == DK - 1)
            end(last)

        transposed("h0T", h0, h0_ready)
        for n in range(4):
            project(n)
        pe.wait_ge(fourier_in, 64)
        for n in range(4):
            wait_done(pe, ("z", n))
        for r in range(TILES):
            for gg in range(2):
                key = ("PQ", r, gg)
                begin(key)
                for g in range(2):
                    last = mm(bank(key, g * 256, (g + 1) * 256), zaT[:, 2 * gg + g, r * P:(r + 1) * P], chan[:],
                              True, True)
                end(last)
        for r in range(TILES):
            for gg in range(2):
                wait_done(pe, ("PQ", r, gg))
        for g in range(4):
            key = ("Y", g)
            begin(key)
            for r in range(TILES):
                mm(bank(key), pq[:, r, g, 0:P], cos_t[:, r, :], r == 0, False)
                last = mm(bank(key), pq[:, r, g, P:2 * P], sin_t[:, r, :], False, r == TILES - 1)
            end(last)
        for n in range(4, 16):
            project(n)
        for c in range(3):
            w = chunk(("in", VV[0] + c))
            for r in range(TILES):
                key = ("v", c, r)
                begin(key)
                for k in range(DK):
                    last = mm(bank(key, 0, CHUNK), hT[:, k, r * P:(r + 1) * P], w[:, k, :], k == 0, k == DK - 1)
                end(last)
        for n in range(22, 26):
            project(n)
        wait_done(pe, ("z", 25))
        wait_done(pe, ("v", 2, TILES - 1))
        pe.wait_ge(bias_in, 16)

        def two(key, lo, hi):
            b = units.bank[key]
            return ps[:, b:b + 2, :].rearrange("p a b -> p (a b)")[:, lo:hi]

        def raw_scores(i):
            r, h = divmod(i, DIL_HEADS)
            key = ("S", i)
            begin(key)
            rows = slice(HD * (h % 2), HD * (h % 2) + HD)
            toks = slice(r * P, (r + 1) * P)
            mm(two(key, 768, 1024), zT[:, 12 + h, toks], kT[:, h, :], True, True)
            mm(two(key, 0, 512), flip[:], bias[:, h, TILES - 1 - r:2 * TILES - 1 - r, :].rearrange("p j m -> p (j m)"),
               True, False)
            mm(two(key, 512, 768), flip[:], bias[:, h, TABLES - 2:TABLES, :].rearrange("p j m -> p (j m)"), True, False)
            mm(two(key, 0, 512), zT[rows, h // 2, toks], zT[rows, 6 + h // 2, :], False, True)
            for g in (1, 2):
                last = mm(two(key, 384 + 128 * g, 512 + 128 * g), zT[rows, 2 * g + h // 2, toks],
                          zT[rows, 6 + 2 * g + h // 2, toks], False, True)
            end(last)

        def outputs(i):
            r, h = divmod(i, DIL_HEADS)
            key = ("O", i)
            begin(key)
            wait_done(pe, ("T0", i))
            wait_done(pe, ("T1", i))
            for j in range(6):
                tile, g = (j, 0) if j < 4 else (r, j - 3)
                col = g * 256 + (h // 2) * P
                mm(bank(key, 0, P), v_sb[:, tile, col:col + P], probT[:, i % 2, j, :], j == 0, j == 5)
            for m in range(2):
                last = mm(bank(key, P, 2 * P), vm[:, m, h * P:(h + 1) * P], probT[:, i % 2, 6 + m, :], m == 0, m == 1)
            end(last)

        raw_scores(0)
        for i in range(N + 1):
            if i + 1 < N:
                raw_scores(i + 1)
            if i >= 1:
                outputs(i - 1)
            if i < N:
                pe.wait_ge(prob_ready, i + 1)
                for t in range(2):
                    key = (f"T{t}", i)
                    begin(key)
                    for j in range(4):
                        c = 4 * t + j
                        last = nc.tensor.transpose(bank(key, j * P, (j + 1) * P), prob[:, i % 2, c * P:(c + 1) * P], ident[:])
                    end(last)
        wait_done(pe, ("O", N - 1))
        pe.wait_ge(wb_in, 16)
        for j in range(DK):
            jj, cols = j // 2, slice((j % 2) * P, (j % 2 + 1) * P)
            for b in range(3):
                w = chunk(("in", GA[0] + 4 * b + jj))
                key = ("G", j, b)
                begin(key)
                for k in range(DK):
                    last = mm(bank(key), w[:, k, cols], hT[:, k, :], k == 0, k == DK - 1)
                end(last)
            w = chunk(("wy", jj))
            for b, (src, n) in enumerate(((oA, 4), (oB, 2), (oC, 4))):
                key = ("Yo", j, b)
                begin(key)
                for k in range(n):
                    lhsT = wb[:, k, j * P:(j + 1) * P] if b == 1 else w[:, 2 * b + k, cols]
                    last = mm(bank(key), lhsT, src[:, k, :], k == 0, k == n - 1)
                end(last)
        wait_done(pe, ("Yo", DK - 1, 2))
        for c in range(4):
            w = chunk(("o", c))
            for r in range(TILES):
                key = ("WO", c, r)
                begin(key)
                for k in range(DK):
                    last = mm(bank(key, 0, CHUNK), merged[:, k, r * P:(r + 1) * P], w[:, k, :], k == 0, k == DK - 1)
                end(last)
        transposed("h1T", h1, h1_ready)

        def key_scores(n):
            wait_done(pe, ("Q", n))
            for q in range(2):
                key = ("SC", n, q)
                begin(key)
                for rr in range(2):
                    r = 2 * q + rr
                    last = mm(bank(key, rr * 256, (rr + 1) * 256), qT[:, n % 2, r * P:(r + 1) * P], KK[:], True, True)
                end(last)

        for n in range(8):
            w = chunk(("pq", n // 2))
            key = ("Q", n)
            begin(key)
            for k in range(DK):
                last = mm(bank(key), w[:, k, (n % 2) * P:(n % 2 + 1) * P], hT[:, k, :], k == 0, k == DK - 1)
            end(last)
            if n >= 1:
                key_scores(n - 1)
        key_scores(7)

    @block.scalar
    def _(sca):
        done = emptied["act"]

        def take(key, dst, src, func=ACT.Copy, **kw):
            wait_full(sca, key)
            nc.scalar.activation(dst, src, func, **kw).then_inc(done, 1)

        for m in range(2):
            for q in range(2):
                take(("memT", m, q), memT[:, 4 * q:4 * q + 4, m * P:(m + 1) * P],
                     bank(("memT", m, q)).rearrange("p (a b) -> p a b", a=4))
        for n in range(4):
            take(("kT", n), kT[:, n, :], bank(("kT", n), 0, MEM))
        for c in range(2):
            for m in range(2):
                take(("vm", c, m), vm[:, m, c * CHUNK:(c + 1) * CHUNK], bank(("vm", c, m), 0, CHUNK))
        take(("bT",), bT[:], bank(("bT",), 0, 50))
        wait_done(sca, ("bT",))
        wait_done(sca, ("beta", 5))
        for r in range(TILES):
            for q in range(2):
                take(("h0T", r, q), hT[:, 4 * q:4 * q + 4, r * P:(r + 1) * P],
                     bank(("h0T", r, q)).rearrange("p (a b) -> p a b", a=4))
        for n in range(4):
            take(("z", n), zaT[:, n, :], bank(("z", n)), ACT.Identity, bias=bT[:, n:n + 1])
        for g in range(4):
            take(("Y", g), oA[:, g, :], bank(("Y", g)))
        for n in list(range(4, 16)) + list(range(22, 26)):
            at = n - 4 if n < 16 else n - 10
            take(("z", n), zT[:, at, :], bank(("z", n)), ACT.Identity, bias=bT[:, n:n + 1])

        def two(key, lo, hi):
            b = units.bank[key]
            return ps[:, b:b + 2, :].rearrange("p a b -> p (a b)")[:, lo:hi]

        def exps(i):
            sca.wait_ge(nm_ready, i + 1)
            if i >= 2:
                wait_full(sca, ("T1", i - 2))
            key = ("S", i)
            nc.scalar.activation(prob[:, i % 2, 0:768], two(key, 0, 768), ACT.Exp, scale=SCALE_B,
                                 bias=nm[:, i % 2, 0:1], accum_out=sums[:, i % 2, 0:1]).then_inc(exp_ready, 1)
            nc.scalar.activation(prob[:, i % 2, 768:1024], two(key, 768, 1024), ACT.Exp, scale=SCALE_C,
                                 bias=nm[:, i % 2, 1:2], accum_out=sums[:, i % 2, 1:2]).then_inc(done, 1)

        exps(0)
        for i in range(N):
            if i + 1 < N:
                exps(i + 1)
            if i >= 2:
                wait_full(sca, ("O", i - 2))
            take(("T0", i), probT[:, i % 2, 0:4, :], bank(("T0", i)).rearrange("p (a b) -> p a b", a=4))
        for j in range(DK):
            for b in range(3):
                key = ("G", j, b)
                if j >= 1:
                    wait_done(sca, ("Yo", j - 1, b))
                take(key, sig[:, b, :], bank(key), ACT.Sigmoid, bias=bT[:, 26 + 8 * b + j:27 + 8 * b + j])
        for r in range(TILES):
            for q in range(2):
                take(("h1T", r, q), hT[:, 4 * q:4 * q + 4, r * P:(r + 1) * P],
                     bank(("h1T", r, q)).rearrange("p (a b) -> p a b", a=4))
        for n in range(8):
            if n >= 2:
                wait_full(sca, ("SC", n - 2, 1))
            take(("Q", n), qT[:, n % 2, :], bank(("Q", n)))

    @block.vector
    def _(dve):
        done = emptied["dve"]
        n_steps = [0]

        def link(*ins):
            for x in ins:
                x.then_inc(dve_step, 1)
            n_steps[0] += len(ins)
            dve.wait_ge(dve_step, n_steps[0])

        def layer_norm(h, ready, gain_value, in_wait):
            for r in range(TILES):
                in_wait(r)
                for j in range(2):
                    nc.vector.bn_stats(stats[:, r, j, :], h[:, r, j * 512:(j + 1) * 512]).then_inc(dve_step, 1)
                n_steps[0] += 2
            dve.wait_ge(dve_step, n_steps[0])
            link(*[nc.vector.bn_aggr(moments[:, r, :], stats[:, r, :, :].rearrange("p a b -> p (a b)"))
                   for r in range(TILES)])
            link(nc.vector.tensor_scalar(rs[:, 0, :], moments[:, :, 1], EPS, None, ALU.add))
            link(nc.vector.tensor_scalar(rs[:, 1, :].bitcast(I32), rs[:, 0, :].bitcast(I32), 1, None,
                                         ALU.arith_shift_right))
            link(nc.vector.tensor_scalar(rs[:, 2, :].bitcast(I32), rs[:, 1, :].bitcast(I32), -1.0, RSQRT_GUESS,
                                         ALU.mult, ALU.add))
            for _ in range(3):
                link(nc.vector.tensor_tensor(rs[:, 3, :], rs[:, 2, :], rs[:, 2, :], ALU.mult))
                link(nc.vector.tensor_tensor(rs[:, 3, :], rs[:, 3, :], rs[:, 0, :], ALU.mult))
                link(nc.vector.tensor_scalar(rs[:, 4, :], rs[:, 3, :], -0.5, 1.5, ALU.mult, ALU.add))
                link(nc.vector.tensor_tensor(rs[:, 2, :], rs[:, 2, :], rs[:, 4, :], ALU.mult))
            dve.wait_ge(gain_in, gain_value)
            for r in range(TILES):
                link(nc.vector.tensor_scalar(h[:, r, :], h[:, r, :], moments[:, r, 0:1], rs[:, 2, r:r + 1],
                                             ALU.subtract, ALU.mult))
                link(nc.vector.tensor_tensor(h[:, r, :], h[:, r, :], gains[:, 0, :], ALU.mult))
                nc.vector.tensor_tensor(h[:, r, :], h[:, r, :], gains[:, 1, :], ALU.add).then_inc(ready, 1)

        layer_norm(h0, h0_ready, 32, lambda r: dve.wait_ge(x_in, 16 * TILES))
        wait_full(dve, ("KK",))
        nc.vector.tensor_copy(KK[0:HD, 0:P], bank(("KK",), 0, P)[0:HD])
        nc.vector.tensor_copy(KK[HD:P, P:2 * P], bank(("KK",), 0, P)[HD:P]).then_inc(done, 1)
        dve.wait_ge(mask_in, 16)
        cuts = [0, 512, 1024, 1536, 1792, 2048, 2304]
        for b in range(6):
            key = ("beta", b)
            wait_full(dve, key)
            lo, hi = cuts[b], cuts[b + 1]
            nc.vector.scalar_tensor_tensor(out=beta[:, lo:hi], in0=ps[0:DIL_HEADS, units.bank[key], 0:hi - lo],
                                           scalar=1.0 / SCALE_B, in1=mask2[:, lo:hi], op0=ALU.mult,
                                           op1=ALU.add).then_inc(done, 1)
        for r in range(TILES):
            for gg in range(2):
                key = ("PQ", r, gg)
                wait_full(dve, key)
                nc.vector.tensor_copy(pq[:, r, 2 * gg:2 * gg + 2, :], bank(key).rearrange("p (g c) -> p g c", g=2)
                                      ).then_inc(done, 1)
        dve.wait_ge(fourier_in, 64)
        for c in range(3):
            for r in range(TILES):
                key = ("v", c, r)
                wait_full(dve, key)
                nc.vector.tensor_tensor(v_sb[:, r, c * CHUNK:(c + 1) * CHUNK], bank(key, 0, CHUNK),
                                        v_bias[:, c * CHUNK:(c + 1) * CHUNK], ALU.add).then_inc(done, 1)

        def two(key, lo, hi):
            b = units.bank[key]
            return ps[:, b:b + 2, :].rearrange("p a b -> p (a b)")[:, lo:hi]

        def maxima(i):
            key = ("S", i)
            wait_full(dve, key)
            if i >= 2:
                wait_done(dve, ("S", i - 2))
            link(nc.vector.tensor_reduce(mx[:, i % 2, 0:1], two(key, 0, 768), AX.X, ALU.max),
                 nc.vector.tensor_reduce(mx[:, i % 2, 1:2], two(key, 768, 1024), AX.X, ALU.max))
            nc.vector.tensor_scalar(nm[:, i % 2, 0:1], mx[:, i % 2, 0:1], -SCALE_B, None, ALU.mult)
            nc.vector.tensor_scalar(nm[:, i % 2, 1:2], mx[:, i % 2, 1:2], -SCALE_C, None, ALU.mult).then_inc(nm_ready, 1)

        def normalise(i):
            wait_done(dve, ("S", i))
            dve.wait_ge(exp_ready, i + 1)
            link(nc.vector.reciprocal(rinv[:, i % 2, :], sums[:, i % 2, :]))
            nc.vector.tensor_scalar(prob[:, i % 2, 0:768], prob[:, i % 2, 0:768], rinv[:, i % 2, 0:1], None, ALU.mult)
            nc.vector.tensor_scalar(prob[:, i % 2, 768:1024], prob[:, i % 2, 768:1024], rinv[:, i % 2, 1:2], None,
                                    ALU.mult).then_inc(prob_ready, 1)

        def take_outputs(i):
            r, h = divmod(i, DIL_HEADS)
            key = ("O", i)
            wait_full(dve, key)
            rows = slice(HD * (h % 2), HD * (h % 2) + HD)
            nc.vector.tensor_copy(oB[rows, h // 2, r * P:(r + 1) * P], bank(key, 0, P)[rows])
            nc.vector.tensor_copy(oC[:, h, r * P:(r + 1) * P], bank(key, P, 2 * P)).then_inc(done, 1)

        dve.wait_ge(beta_out, 16)
        maxima(0)
        for i in range(N + 1):
            if i < N:
                normalise(i)
            if i + 1 < N:
                maxima(i + 1)
            if i >= 1:
                take_outputs(i - 1)
            if i < N:
                if i >= 2:
                    wait_full(dve, ("O", i - 2))
                wait_full(dve, ("T1", i))
                nc.vector.tensor_copy(probT[:, i % 2, 4:8, :], bank(("T1", i)).rearrange("p (a b) -> p a b", a=4)
                                      ).then_inc(done, 1)
        for j in range(DK):
            for b in range(3):
                key = ("Yo", j, b)
                wait_full(dve, key)
                wait_done(dve, ("G", j, b))
                if b == 0:
                    nc.vector.tensor_tensor(merged[:, j, :], sig[:, b, :], bank(key), ALU.mult).then_inc(done, 1)
                    wait_done(dve, key)
                else:
                    nc.vector.tensor_tensor(part[:, b - 1, :], sig[:, b, :], bank(key), ALU.mult).then_inc(dve_step, 1)
                    n_steps[0] += 1
                    dve.wait_ge(dve_step, n_steps[0])
                    nc.vector.tensor_tensor(merged[:, j, :], merged[:, j, :], part[:, b - 1, :], ALU.add).then_inc(done, 1)
                    wait_done(dve, key)
        for c in range(4):
            for r in range(TILES):
                key = ("WO", c, r)
                wait_full(dve, key)
                nc.vector.scalar_tensor_tensor(out=h1[:, r, c * CHUNK:(c + 1) * CHUNK],
                                               in0=h0[:, r, c * CHUNK:(c + 1) * CHUNK], scalar=ALPHA,
                                               in1=bank(key, 0, CHUNK), op0=ALU.mult, op1=ALU.add).then_inc(done, 1)
        wait_done(dve, ("WO", 3, TILES - 1))
        layer_norm(h1, h1_ready, 64, lambda r: None)
        for n in range(8):
            for q in range(2):
                key = ("SC", n, q)
                wait_full(dve, key)
                for rr in range(2):
                    ins = nc.vector.tensor_copy(scores[:, (2 * q + rr) * 8 + n, :], bank(key, rr * 256, (rr + 1) * 256))
                ins.then_inc(done, 1)


def build_peer(nc, h1, scores, u_tab, v_tab, ident, ln2_g, ln2_b, out_rows):
    RING = 8
    LEAD = 2
    with ExitStack() as ctx:
        def sb(name, shape, dt=F32):
            return ctx.enter_context(nc.sbuf_tensor("peer_" + name, shape, dt))

        def sem(name):
            return ctx.enter_context(nc.semaphore("peer_" + name))

        u_ring = sb("u_ring", [P, RING, D])
        v_ring = sb("v_ring", [P, RING, D])
        x_cur = sb("x_cur", [P, D])
        y_sb = sb("y_sb", [P, D])
        out_sb = sb("out_sb", [P, D])
        diag = sb("diag", [P, TOPK, P])
        gain = sb("gain", [P, D])
        shift = sb("shift", [P, D])
        s12 = sb("s12", [P, 2 * KEYS])
        s12b = sb("s12b", [P, 2 * KEYS])
        v12 = sb("v12", [P, 2, TOPK])
        i12 = sb("i12", [P, 2, TOPK], U32)
        cand = sb("cand", [P, TOPK, TOPK])
        candb = sb("candb", [P, TOPK, TOPK])
        best = sb("best", [P, TOPK])
        pos = sb("pos", [P, TOPK], U32)
        ab = sb("ab", [P, 2, TOPK], U32)
        iota_f = sb("iota_f", [P, TOPK])
        iota_u = sb("iota_u", [P, TOPK], U32)
        pick = sb("pick", [P, 2, TOPK, TOPK])
        e12 = sb("e12", [P, 2, TOPK])
        expert_all = sb("expert_all", [P, STEPS, TOPK], U32)
        expert_u = sb("expert_u", [P, 2, TOPK], U32)
        expert_v = sb("expert_v", [P, 2, TOPK], U32)
        neg_max = sb("neg_max", [P, 1])
        gate_all = sb("gate_all", [P, STEPS, TOPK])
        gate_sum = sb("gate_sum", [P, STEPS])
        dots = sb("dots", [P, TOPK])
        act = sb("act", [P, TOPK])
        rinv = sb("rinv", [P, 1])
        coef = sb("coef", [P, TOPK])
        stats = sb("stats", [P, 2, 6])
        moments = sb("moments", [P, 2])
        rs = sb("rs", [P, 6])
        y_ps = ctx.enter_context(nc.psum_tensor("y_ps", [P, 2, 512], F32))

        u_landed = [sem(f"u_landed{j}") for j in range(RING)]
        v_landed = [sem(f"v_landed{j}") for j in range(RING)]
        u_used, v_used = sem("u_used"), sem("v_used")
        expert_ready, expert_copied = sem("expert_ready"), sem("expert_copied")
        scores_staged = sem("scores_staged")
        best_ready, gate_ready = sem("best_ready"), sem("gate_ready")
        act_ready, coef_ready, diag_ready = sem("act_ready"), sem("coef_ready"), sem("diag_ready")
        y_copied = sem("y_copied")
        out_ready, out_moved = sem("out_ready"), sem("out_moved")
        consts_ready, dve_step = sem("consts_ready"), sem("dve_step")
        dve_passed, pool_passed = sem("dve_passed"), sem("pool_passed")

        block = ctx.enter_context(nc.Block())

        @block.gpsimd
        def _(pool):
            nc.gpsimd.iota(iota_u[:], [[1, TOPK]], base=0, channel_multiplier=0).then_inc(consts_ready, 1)
            pool.wait_ge(consts_ready, 1)
            nc.gpsimd.tensor_copy(iota_f[:], iota_u[:]).then_inc(consts_ready, 1)

            def gather(ring, slot, table, index, landed):
                return nc.gpsimd.indirect_dma_start(
                    out=ring[:, slot, :], out_offset=None, in_=table,
                    in_offset=bass.IndirectOffsetOnAxis(ap=index, axis=0),
                ).then_inc(landed[slot], 16)

            def u_rows(s, k, first, b):
                if k >= RING or not first:
                    pool.wait_ge(u_used, s * TOPK + (k - RING + 1))
                    pool.sem_inc(pool_passed)
                gather(u_ring, k % RING, u_tab, expert_u[:, b, k:k + 1], u_landed)

            def v_rows(s, k, first, b):
                if k >= RING or not first:
                    pool.wait_ge(v_used, s * TOPK + (k - RING + 1))
                    pool.sem_inc(pool_passed)
                gather(v_ring, k % RING, v_tab, expert_v[:, b, k:k + 1], v_landed)

            def stage(s, table_step, stage_buf):
                src = expert_all[:, table_step, :] if isinstance(table_step, int) else \
                    expert_all[:, bass.ds(table_step, 1), :].rearrange("p a k -> p (a k)")
                nc.gpsimd.tensor_copy(stage_buf, src).then_inc(expert_copied, 1)

            def landed(sems, s):
                for j in range(RING):
                    pool.wait_ge(sems[j], s * 32 + 32)
                pool.sem_inc(pool_passed)

            pool.wait_ge(expert_ready, 1)
            stage(0, 0, expert_u[:, 0, :])
            pool.wait_ge(expert_copied, 1)
            for k in range(TOPK):
                u_rows(0, k, True, 0)

            def both(s, b, first=False, second=False):
                pool.wait_ge(expert_ready, s + 2)
                pool.sem_inc(pool_passed)
                if not first:
                    landed(u_landed, s - 1)
                    if not second:
                        landed(v_landed, s - 2)
                stage(s, s + 1, expert_u[:, 1 - b, :])
                stage(s, s, expert_v[:, b, :])
                pool.wait_ge(expert_copied, s * 2 + 3)
                pool.sem_inc(pool_passed)
                for k in range(TOPK):
                    u_rows(s + 1, k, False, 1 - b)
                    v_rows(s, k, first, b)

            both(0, 0, first=True)
            both(1, 1, second=True)
            both(2, 0)
            with pool.Fori(0, (STEPS - 4) // 2) as pair:
                both(pair * 2 + 3, 1)
                both(pair * 2 + 4, 0)
            last = STEPS - 1
            landed(v_landed, last - 2)
            stage(last, last, expert_v[:, 1, :])
            pool.wait_ge(expert_copied, last * 2 + 2)
            for k in range(TOPK):
                v_rows(last, k, False, 1)

        @block.scalar
        def _(sca):
            sca.wait_ge(consts_ready, 2)

            def at(t, s):
                return t[:, bass.ds(s, 1), :].rearrange("p a k -> p (a k)") if not isinstance(s, int) else t[:, s, :]

            def stage_scores(s):
                nc.scalar.copy(s12[:], at(scores, s)).then_inc(scores_staged, 1)

            def gates(s):
                sca.wait_ge(best_ready, s + 1)
                nc.scalar.activation(at(gate_all, s), best[:], ACT.Exp, bias=neg_max[:, 0:1],
                                     accum_out=gate_sum[:, bass.ds(s, 1)]).then_inc(gate_ready, 1)

            def activate(s):
                sca.wait_ge(u_used, s * TOPK + TOPK)
                if not (isinstance(s, int) and s == 0):
                    sca.wait_ge(coef_ready, s)
                nc.scalar.activation(act[:], dots[:], ACT.Gelu).then_inc(act_ready, 1)

            def diagonals(s):
                sca.wait_ge(coef_ready, s + 1)
                for k in range(TOPK):
                    if not (isinstance(s, int) and s == 0):
                        sca.wait_ge(v_used, s * TOPK + (k - TOPK + 1))
                    nc.scalar.activation(diag[:, k, :], ident[:], ACT.Copy, scale=coef[:, k:k + 1]).then_inc(diag_ready, 1)

            def copy_y(t):
                sca.wait_ge(v_used, (t + 1) * HEADS * TOPK)
                nc.scalar.copy(y_sb[:], y_ps[:].rearrange("p a b -> p (a b)")).then_inc(y_copied, 1)

            def step(s, ahead, copy_tile=None):
                if ahead:
                    stage_scores(s + LEAD)
                activate(s)
                if copy_tile is not None:
                    copy_y(copy_tile)
                diagonals(s)
                if ahead:
                    gates(s + LEAD)

            for s in range(LEAD):
                stage_scores(s)
                gates(s)
            step(0, True)
            with sca.Fori(1, HEADS) as s:
                step(s, True)
            with sca.Fori(1, TILES - 1) as t:
                step(t * HEADS, True, t - 1)
                with sca.Fori(1, HEADS) as h:
                    step(t * HEADS + h, True)
            step((TILES - 1) * HEADS, True, TILES - 2)
            with sca.Fori((TILES - 1) * HEADS + 1, STEPS - LEAD) as s:
                step(s, True)
            for s in range(STEPS - LEAD, STEPS):
                step(s, False)
            copy_y(TILES - 1)

        @block.tensor
        def _(pe):
            def products(s, first_step, start):
                for k in range(TOPK):
                    pe.wait_ge(diag_ready, s * TOPK + k + 1)
                    pe.wait_ge(v_landed[k % RING], s * 32 + 16 * (k // RING) + 16)
                    for half in range(2):
                        mm = nc.tensor.matmul(y_ps[:, half, :], diag[:, k, :],
                                              v_ring[:, k % RING, half * 512:(half + 1) * 512],
                                              start=start and k == 0, stop=False, skip_group_check=True)
                    mm.then_inc(v_used, 1)
                    last = mm
                return last

            products(0, True, True)
            with pe.Fori(1, HEADS) as h:
                products(h, False, False)
            with pe.Fori(1, TILES) as t:
                pe.wait_ge(y_copied, t)
                products(t * HEADS, False, True)
                with pe.Fori(1, HEADS) as h:
                    products(t * HEADS + h, False, False)
    
        @block.vector
        def _(dve):
            dve.wait_ge(consts_ready, 2)
            links = {"n": 0}
            PER_TOP = 9
            PER_COEF = 1

            class Chain:
                def __init__(self, base):
                    self.base, self.n = base, 0

                def after(self, *ins):
                    for x in ins:
                        x.then_inc(dve_step, 1)
                        self.n += 1
                    dve.wait_ge(dve_step, self.base + self.n)
                    dve.sem_inc(dve_passed)

            def at(t, s):
                return t[:, bass.ds(s, 1), :].rearrange("p a k -> p (a k)") if not isinstance(s, int) else t[:, s, :]

            def load_tile(t, c):
                c.after(nc.vector.tensor_copy(x_cur[:], at(h1, t)))

            def dot_products(s):
                if not (isinstance(s, int) and s == 0):
                    dve.wait_ge(act_ready, s)
                for k in range(TOPK):
                    dve.wait_ge(u_landed[k % RING], s * 32 + 16 * (k // RING) + 16)
                    row = u_ring[:, k % RING, :]
                    nc.vector.tensor_tensor_reduce(row, row, x_cur[:], 1.0, 0.0, ALU.mult, ALU.add,
                                                   dots[:, k:k + 1]).then_inc(u_used, 1)

            def top_halves(s, c):
                dve.wait_ge(scores_staged, s + 1)
                dve.sem_inc(dve_passed)
                for r in range(2):
                    lo, hi = 8 * r, 8 * r + 8
                    src = s12 if r == 0 else s12b
                    c.after(*[nc.vector.max(v12[:, x, lo:hi], src[:, x * KEYS:(x + 1) * KEYS]) for x in range(2)])
                    ins = [nc.vector.max_index(i12[:, x, lo:hi], v12[:, x, lo:hi], src[:, x * KEYS:(x + 1) * KEYS])
                           for x in range(2)]
                    if r == 0:
                        ins += [nc.vector.match_replace(s12b[:, x * KEYS:(x + 1) * KEYS], v12[:, x, lo:hi],
                                                        src[:, x * KEYS:(x + 1) * KEYS], LOWEST) for x in range(2)]
                    c.after(*ins)
            def top_pairs(s, c):
                c.after(nc.vector.tensor_tensor(cand[:], v12[:, 0, :].unsqueeze(2).broadcast_to([P, TOPK, TOPK]),
                                                v12[:, 1, :].unsqueeze(1).broadcast_to([P, TOPK, TOPK]), ALU.add))
                if not (isinstance(s, int) and s == 0):
                    dve.wait_ge(gate_ready, s)
                    dve.sem_inc(dve_passed)
                for r in range(2):
                    lo, hi = 8 * r, 8 * r + 8
                    src = (cand if r == 0 else candb)[:].rearrange("p a b -> p (a b)")
                    c.after(nc.vector.max(best[:, lo:hi], src))
                    ins = [nc.vector.max_index(pos[:, lo:hi], best[:, lo:hi], src)]
                    if r == 0:
                        ins += [nc.vector.match_replace(candb[:].rearrange("p a b -> p (a b)"), best[:, lo:hi], src, LOWEST)]
                    c.after(*ins)
                c.after(nc.vector.tensor_scalar(ab[:, 0, :], pos[:], 4, None, ALU.logical_shift_right),
                        nc.vector.tensor_scalar(ab[:, 1, :], pos[:], TOPK - 1, None, ALU.bitwise_and),
                        )
                nc.vector.tensor_scalar(neg_max[:], best[:, 0:1], -1.0, None, ALU.mult).then_inc(best_ready, 1)
                c.after(nc.vector.tensor_tensor(
                    pick[:].rearrange("p x k a -> p (x k) a"),
                    ab[:].rearrange("p x k -> p (x k)").unsqueeze(2).broadcast_to([P, 2 * TOPK, TOPK]),
                    iota_f[:].unsqueeze(1).broadcast_to([P, 2 * TOPK, TOPK]), ALU.is_equal))
                c.after(nc.vector.tensor_tensor(
                    pick[:], pick[:], i12[:].unsqueeze(2).broadcast_to([P, 2, TOPK, TOPK]), ALU.mult))
                c.after(nc.vector.tensor_reduce(e12[:], pick[:], AX.X, ALU.add))
                nc.vector.scalar_tensor_tensor(out=at(expert_all, s), in0=e12[:, 0, :], scalar=float(KEYS),
                                               in1=e12[:, 1, :], op0=ALU.mult, op1=ALU.add).then_inc(expert_ready, 1)

            def coefficients(s, c):
                dve.wait_ge(gate_ready, s + 1)
                c.after(nc.vector.reciprocal(rinv[:], gate_sum[:, bass.ds(s, 1)]))
                dve.wait_ge(act_ready, s + 1)
                if not (isinstance(s, int) and s == 0):
                    dve.wait_ge(diag_ready, s * TOPK)
                nc.vector.scalar_tensor_tensor(out=coef[:], in0=at(gate_all, s), scalar=rinv[:, 0:1],
                                               in1=act[:], op0=ALU.mult, op1=ALU.mult).then_inc(coef_ready, 1)

            def finish(t, c):
                dve.wait_ge(y_copied, t + 1)
                c.after(nc.vector.scalar_tensor_tensor(out=y_sb[:], in0=at(h1, t), scalar=ALPHA, in1=y_sb[:],
                                                       op0=ALU.mult, op1=ALU.add))
                c.after(*[nc.vector.bn_stats(stats[:, j, :], y_sb[:, j * 512:(j + 1) * 512]) for j in range(2)])
                c.after(nc.vector.bn_aggr(moments[:], stats[:].rearrange("p a b -> p (a b)")))
                c.after(nc.vector.tensor_scalar(rs[:, 0:1], moments[:, 1:2], EPS, None, ALU.add))
                c.after(nc.vector.tensor_scalar(rs[:, 1:2].bitcast(I32), rs[:, 0:1].bitcast(I32), 1, None,
                                                ALU.arith_shift_right))
                c.after(nc.vector.tensor_scalar(rs[:, 2:3].bitcast(I32), rs[:, 1:2].bitcast(I32), -1.0, RSQRT_GUESS,
                                                ALU.mult, ALU.add))
                for _ in range(3):
                    c.after(nc.vector.scalar_tensor_tensor(out=rs[:, 3:4], in0=rs[:, 2:3], scalar=rs[:, 0:1],
                                                           in1=rs[:, 2:3], op0=ALU.mult, op1=ALU.mult))
                    c.after(nc.vector.tensor_scalar(rs[:, 4:5], rs[:, 3:4], -0.5, 1.5, ALU.mult, ALU.add))
                    c.after(nc.vector.tensor_tensor(rs[:, 2:3], rs[:, 2:3], rs[:, 4:5], ALU.mult))
                c.after(nc.vector.tensor_scalar(y_sb[:], y_sb[:], moments[:, 0:1], rs[:, 2:3],
                                                ALU.subtract, ALU.mult))
                dve.wait_ge(out_moved, t * 16 + 32)
                c.after(nc.vector.tensor_tensor(out_sb[:], y_sb[:], gain[:], ALU.mult))
                nc.vector.tensor_tensor(out_sb[:], out_sb[:], shift[:], ALU.add).then_inc(out_ready, 1)

            TOP = 21
            FIN = 18

            def top(s, base, c=None):
                c = Chain(base)
                top_halves(s, c)
                top_pairs(s, c)
                assert c.n == TOP, c.n

            STEP = TOP + 1

            def step(s, base, ahead):
                dot_products(s)
                c = Chain(base)
                if ahead:
                    top_halves(s + LEAD, c)
                coefficients(s, c)
                if ahead:
                    top_pairs(s + LEAD, c)
                assert c.n == (STEP if ahead else 1), c.n
                return base + c.n

            def closing(t, base):
                c = Chain(base)
                finish(t, c)
                assert c.n == FIN, c.n
                return base + FIN

            def opening(t, base):
                c = Chain(base)
                load_tile(t, c)
                return base + 1

            base = 0
            for s in range(LEAD):
                top(s, base)
                base += TOP
            base = opening(0, base)
            base = step(0, base, True)
            with dve.Fori(1, HEADS) as s:
                step(s, base + (s - 1) * STEP, True)
            base += (HEADS - 1) * STEP
            TILE = 1 + HEADS * STEP + FIN
            with dve.Fori(1, TILES - 1) as t:
                b = base + (t - 1) * TILE
                opening(t, b)
                with dve.Fori(0, 2) as h:
                    step(t * HEADS + h, b + 1 + h * STEP, True)
                closing(t - 1, b + 1 + 2 * STEP)
                with dve.Fori(2, HEADS) as h:
                    step(t * HEADS + h, b + 1 + FIN + h * STEP, True)
            base += (TILES - 2) * TILE
            t = TILES - 1
            base = opening(t, base)
            with dve.Fori(0, 2) as h:
                step(t * HEADS + h, base + h * STEP, True)
            base += 2 * STEP
            base = closing(t - 1, base)
            with dve.Fori(2, HEADS - LEAD) as h:
                step(t * HEADS + h, base + (h - 2) * STEP, True)
            base += (HEADS - LEAD - 2) * STEP
            for s in range(STEPS - LEAD, STEPS):
                base = step(s, base, False)
            base = closing(t, base)

        @block.sync
        def _(sp):
            row = lambda a: a.rearrange("(a n) -> a n", a=1).broadcast_to([P, D])
            sp.dma_start(gain[:], row(ln2_g[0])).then_inc(out_moved, 16)
            sp.dma_start(shift[:], row(ln2_b[0])).then_inc(out_moved, 16)
            for t in range(TILES):
                sp.wait_ge(out_ready, t + 1)
                sp.dma_start(out_rows[t], out_sb[:]).then_inc(out_moved, 16)
            sp.wait_ge(out_moved, 32 + 16 * TILES)


def t5_bucket(rel):
    half, exact = 16, 8
    n = np.abs(rel)
    nf = np.maximum(n, 1).astype(np.float32)
    large = exact + (np.log(nf / exact) / np.float32(math.log(1024 / exact)) * (half - exact)).astype(np.int32)
    return np.where(rel > 0, half, 0) + np.where(n < exact, n, np.minimum(large, half - 1))

def shape_constants():
    step = np.arange(256) - 127
    onehot = np.zeros((32, 9, 256), np.float32)
    mask = np.zeros((4, 9, 256), np.float32)
    for j in range(9):
        if j < 7:
            rel = 4 * step + (j - 3)
            allowed = np.abs(rel) <= 64
        elif j == 7:
            rel, allowed = 4 * step, np.abs(step) <= 64
        else:
            rel, allowed = 4 * step, step % 4 == 0
        bucket = t5_bucket(rel)
        onehot[bucket, j, np.arange(256)] = 1.0
        mask[:, j, ~allowed] = -1e30
    token = np.arange(512).reshape(128, 4).T.reshape(-1)
    angle = 2 * math.pi / 512 * ((token[:, None] * token[None, :]) % 512)
    ch = np.arange(128)
    phi = 2 * math.pi / 128 * ((ch[:, None] * ch[None, :]) % 128)
    norm = 1.0 / math.sqrt(512 * 128)
    return {
        "c_onehot": onehot.reshape(32, -1),
        "c_mask": mask.reshape(4, -1),
        "c_chan": (np.concatenate([np.cos(phi), np.sin(phi)], 1) * norm).astype(np.float32),
        "c_cos": np.cos(angle).astype(np.float32),
        "c_sin": (-np.sin(angle)).astype(np.float32),
    }


_INS = ["x", "mem", "rel_bias", "ln0_g", "ln0_b", "w_in", "b_in", "w_a", "w_b", "w_c", "w_mem_kv", "w_o",
        "ln1_g", "ln1_b", "w_pq", "sub_keys1", "sub_keys2", "u_tab", "v_tab", "ln2_g", "ln2_b"]


def kernel(**inputs):
    import numpy as _np
    import concourse.bacc as _bacc
    from concourse import mybir as _mybir
    from concourse.bass_utils import run_bass_kernel_spmd as _run

    nc = _bacc.Bacc("TRN2", target_bir_lowering=False, num_devices=1)
    arrays, args = {}, {}
    given = {name: _np.ascontiguousarray(inputs[name]) for name in _INS}
    for name, a in {**given, **shape_constants()}.items():
        arrays[f"in_{name}_dram"] = a
        args[name] = nc.dram_tensor(f"in_{name}_dram", a.shape, _mybir.dt.from_np(a.dtype), kind="ExternalInput").ap()
    args["out"] = nc.dram_tensor("out_0_dram", (1, SEQ, D), F32, kind="ExternalOutput").ap()
    build(nc, **args)
    r = _run(nc, [arrays], core_ids=[0])
    return r.results[0]["out_0_dram"]
```

```python
from contextlib import ExitStack
import math

import numpy as np

import concourse.bass as bass
from concourse import mybir

F32 = mybir.dt.float32
U32 = mybir.dt.uint32
I32 = mybir.dt.int32
ALU = mybir.AluOpType
ACT = mybir.ActivationFunctionType
AX = mybir.AxisListType

P = 128
D = 1024
SEQ = 512
TILES = SEQ // P
GROUPS = 2
GT = TILES // GROUPS
GW = GT * P
DK = D // P
MEM = 256
CHUNK = 256
RING = 4
PEER_RING = 2
BANKS = 8
BUCKETS = 32
DIL_HEADS = 4
HD = 64
DELTAS = 2 * P
TABLES = 2 * TILES - 1 + 2
BETA_CUTS = [0, 512, 1024, 1536, 1792, 2048, 2304]
BETA_GROUP = [0, 0, 0, 0, 1, 2]
SCALE_B = HD ** -0.5
SCALE_C = 128 ** -0.5
ALPHA = 2.0 ** 0.25
EPS = 1e-5
RSQRT_GUESS = float(0x5F3759DF)

HEADS = 8
TOPK = 16
KEYS = 128
STEPS = TILES * HEADS
ROWS = 8
DIAGS = 16
SCORE_SLOTS = 3 * HEADS
LOWEST = -3.0e38

ZA, QK, VV, QC, GA = range(0, 2), range(2, 8), range(8, 11), range(11, 13), range(13, 25)
PAIRS = TILES * DIL_HEADS


BRANCH_ORDER = [(2 * jj + i, b) for jj in range(DK // 2) for b in range(3) for i in range(2)]
BRANCH_AT = {key: n for n, key in enumerate(BRANCH_ORDER)}
SIGS = 4


class Units:

    def __init__(self):
        self.index, self.bank, self.reader, self.ordinal, self.before = {}, {}, {}, {}, {}
        self.emptied = {"act": 0, "dve": 0}
        self.owner = [None] * BANKS
        self.turn, self.turns = 0, BANKS

    def add(self, key, reader, bank=None, width=1):
        if bank is None:
            bank, self.turn = self.turn, (self.turn + 1) % self.turns
        self.before[key] = {self.owner[b] for b in range(bank, bank + width)} - {None}
        for b in range(bank, bank + width):
            self.owner[b] = key
        self.index[key], self.bank[key], self.reader[key] = len(self.index), bank, reader
        self.emptied[reader] += 1
        self.ordinal[key] = self.emptied[reader]


def tail_units(g):
    gates = []
    for n in range(0, len(BRANCH_ORDER), 2):
        two = BRANCH_ORDER[n:n + 2]
        gates += [(("G", g, j, b), "act") for j, b in two] + [(("Yo", g, j, b), "dve") for j, b in two]
    wo = [[(("WO", g, c, r), "dve") for r in range(GT)] for c in range(4)]
    h1t = [(("h1T", g, r, q), "act") for r in range(GT) for q in range(2)]
    q = [[(("Q", g, n), "act")] + ([(("SC", g, n - 1), "dve")] if n >= 2 else []) for n in range(8)]
    q[0].append((("SC", g, 0), "dve"))
    q[7].append((("SC", g, 7), "dve"))
    return gates, wo, h1t, q


def window_units():
    gates, wo, h1t, q = tail_units(1)
    w = {j: gates[6 * j:6 * j + 6] for j in range(DK)}
    w[8], w[9], w[10] = wo[0] + wo[1], wo[2] + wo[3], []
    w[11] = h1t + q[0] + q[1]
    w[12] = q[2] + q[3] + q[4] + q[5]
    w[13] = q[6] + q[7]
    w[14], w[15] = [], []
    return w


def slot_units():
    out = {}
    for w, items in window_units().items():
        for n, (key, _) in enumerate(items):
            out.setdefault((w, 1 + n * 14 // max(len(items), 1)), []).append(key)
    return out


def plan():
    u = Units()
    for m in range(2):
        for q in range(2):
            u.add(("memT", m, q), "act")
    for n in range(4):
        u.add(("kT", n), "act")
    for c in range(2):
        for m in range(2):
            u.add(("vm", c, m), "act")
    u.add(("bT",), "act")
    u.add(("KK",), "dve")
    for b in range(6):
        u.add(("beta", b), "dve")
    for r in range(TILES):
        for q in range(2):
            u.add(("h0T", r, q), "act")
    for n in range(4):
        u.add(("z", n), "act")
    for r in range(TILES):
        for g in range(2):
            u.add(("PQ", r, g), "dve")
    for g in range(4):
        u.add(("Y", g), "act")
    for n in range(4, 16):
        u.add(("z", n), "act")
    for c in range(3):
        for r in range(TILES):
            u.add(("v", c, r), "dve")
    for n in range(22, 26):
        u.add(("z", n), "act")
    u.add(("S", 0), "act", bank=0, width=2)
    for i in range(PAIRS + 1):
        if i + 1 < PAIRS:
            u.add(("S", i + 1), "act", bank=2 * ((i + 1) % 2), width=2)
        if i >= 1:
            u.add(("O", i - 1), "dve", bank=6 + i % 2)
        if i < PAIRS:
            u.add(("T0", i), "act", bank=4)
            u.add(("T1", i), "dve", bank=5)
    u.turn = 0
    gates, wo, h1t, q = tail_units(0)
    for key, reader in gates + sum(wo, []) + h1t + sum(q, []):
        u.add(key, reader)
    u.before["y"] = {u.owner[6], u.owner[7]}
    u.turn, u.turns = 0, 6
    for w in sorted(window_units()):
        for key, reader in window_units()[w]:
            u.add(key, reader)
    return u


def chunk_plan():
    c = []
    for n in range(4):
        c.append((("kv", n), ("kT", 2 * n + 1) if n < 2 else ("vm", n - 2, 1)))
    for n in list(ZA) + list(QK):
        c.append((("in", n), ("z", 2 * n + 1)))
    for n in VV:
        c.append((("in", n), ("v", n - VV[0], TILES - 1)))
    for n in QC:
        c.append((("in", n), ("z", 2 * n + 1)))
    for g in range(GROUPS):
        for jj in range(4):
            for b in range(3):
                c.append((("in", GA[0] + 4 * b + jj, g), ("G", g, 2 * jj + 1, b)))
                c.append((("abc"[b], jj, g), ("Yo", g, 2 * jj + 1, b)))
        for n in range(4):
            c.append((("o", n, g), ("WO", g, n, GT - 1)))
        for n in range(4):
            c.append((("pq", n, g), ("Q", g, 2 * n + 1)))
    first_peer = next(i for i, (key, _) in enumerate(c) if key == ("in", GA[0], 1))
    out, held, loads = [], {}, {}
    for i, (key, last) in enumerate(c):
        slot = i % RING if i < first_peer else (i - first_peer) % PEER_RING
        loads[slot] = loads.get(slot, 0) + 1
        out.append((key, last, slot, held.get(slot), 16 * loads[slot]))
        held[slot] = last
    return out


def build(nc, x, mem, rel_bias, ln0_g, ln0_b, w_in, b_in, w_a, w_b, w_c, w_mem_kv, w_o,
          ln1_g, ln1_b, w_pq, sub_keys1, sub_keys2, u_tab, v_tab, ln2_g, ln2_b,
          c_onehot, c_mask, c_chan, c_cos, c_sin, out):
    beta_dram = nc.dram_tensor("beta_rows", [DIL_HEADS * TABLES, DELTAS], F32).ap()
    beta_copies = nc.dram_tensor("beta_copies", [DIL_HEADS * TABLES, P, DELTAS], F32).ap()
    tile_rows = lambda t: t[0].rearrange("(m r) d -> r m d", r=TILES)
    x_rows, out_rows = tile_rows(x), tile_rows(out)
    units, chunks = plan(), chunk_plan()
    chunk_at = {c[0]: c for c in chunks}
    slots = slot_units()
    ctx = ExitStack()
    with ctx:
        def sb(name, shape, dt=F32):
            return ctx.enter_context(nc.sbuf_tensor(name, shape, dt))

        def sem(name):
            return ctx.enter_context(nc.semaphore(name))

        K = 256
        arena = sb("arena", [P, 178 * K])

        def at(kb, size):
            return arena[:, kb * K:(kb + size) * K]

        h = at(0, 16).rearrange("p (r d) -> p r d", r=TILES)
        hT = at(16, 16).rearrange("p (k s) -> p k s", k=DK)
        gains = at(32, 8).rearrange("p (a d) -> p a d", a=2)
        slot01 = at(40, 16).rearrange("p (s k n) -> p s k n", s=2, k=DK)
        o_1 = at(56, 10).rearrange("p (k s) -> p k s", k=10)
        merged = at(66, 8).rearrange("p (k s) -> p k s", k=DK)
        sig = at(74, 4).rearrange("p (b s) -> p b s", b=SIGS)
        part = at(78, 2).rearrange("p (b s) -> p b s", b=2)
        qT = at(80, 2).rearrange("p (b s) -> p b s", b=2)
        scores = at(82, 24).rearrange("p (s k) -> p s k", s=SCORE_SLOTS)
        u_ring = at(106, 32).rearrange("p (j d) -> p j d", j=ROWS)
        v_ring = at(138, 32).rearrange("p (j d) -> p j d", j=ROWS)
        diag = at(170, 8).rearrange("p (j q) -> p j q", j=DIAGS)
        slot23 = at(162, 16).rearrange("p (s k n) -> p s k n", s=2, k=DK)
        o_0 = at(152, 10).rearrange("p (k s) -> p k s", k=10)
        zT = at(106, 32).rearrange("p (t s) -> p t s", t=16)
        kT = at(138, 4).rearrange("p (t s) -> p t s", t=4)
        vm = at(142, 4).rearrange("p (m n) -> p m n", m=2)
        v_sb = at(94, 12).rearrange("p (r n) -> p r n", r=TILES)
        B0 = DIL_HEADS * TABLES * P
        bias = arena[:, 66 * K:66 * K + B0].rearrange("p (h j m) -> p h j m", h=DIL_HEADS, j=TABLES)
        prob = at(84, 8).rearrange("p (b k) -> p b k", b=2)
        probT_t = sb("probT", [P, 2, 8, P])
        probT = probT_t[:]
        zaT = at(66, 8).rearrange("p (g s) -> p g s", g=4)
        pq = at(74, 16).rearrange("p (r g c) -> p r g c", r=TILES, g=4)
        cos_t = zT[:, 0:4, :]
        sin_t = zT[:, 4:8, :]
        memT = zT[:, 8:12, :].rearrange("p a (b m) -> p (a b) m", m=MEM)
        mem_sb = zT[:, 12:16, :].rearrange("p (m a) b -> p m (a b)", m=2)
        onehot = zT[0:BUCKETS, 0:5, :].rearrange("p a b -> p (a b)")[:, 0:TABLES * DELTAS]
        mask = hT[0:DIL_HEADS, 0:5, :].rearrange("p a b -> p (a b)")[:, 0:TABLES * DELTAS]
        beta = o_1[0:DIL_HEADS, :, :].rearrange("p a b -> p (a b)")[:, 0:TABLES * DELTAS]
        o = [o_0, o_1]
        y_sb = probT_t[:].rearrange("p b j q -> p (b j q)")[:, 0:D]

        ident = sb("ident", [P, P])
        KK = sb("KK", [P, 2 * P])
        bT = sb("bT", [P, 50])
        early = sb("early", [P, 768 + 256 + 128 + 128 + 12])
        v_bias, chan = early[:, 0:768], early[:, 768:1024]
        keys, b_rows = early[:, 1024:1152], early[0:50, 1152:1280]
        relb = early[0:BUCKETS, 1280:1292]
        stats = sb("stats", [P, GT, 2, 6])
        moments = sb("moments", [P, TILES, 2])
        rs = sb("rs", [P, 5, TILES])
        mx, nm = sb("mx", [P, 2, 3]), sb("nm", [P, 2, 2])
        sums, rinv = sb("sums", [P, 2, 2]), sb("rinv", [P, 2, 2])

        s12 = early[:, 0:256]
        s12b = early[:, 256:512]
        cand = early[:, 512:768].rearrange("p (a b) -> p a b", a=TOPK)
        candb = early[:, 768:1024].rearrange("p (a b) -> p a b", a=TOPK)
        pick = sb("pick", [P, 2, TOPK, TOPK])
        v12, i12 = sb("v12", [P, 2, TOPK]), sb("i12", [P, 2, TOPK], U32)
        best, pos = sb("best", [P, TOPK]), sb("pos", [P, TOPK], U32)
        ab = sb("ab", [P, 2, TOPK], U32)
        iota_f, iota_u = sb("iota_f", [P, TOPK]), sb("iota_u", [P, TOPK], U32)
        e12 = sb("e12", [P, 2, TOPK])
        expert_all = sb("expert_all", [P, STEPS, TOPK], U32)
        expert_u, expert_v = sb("expert_u", [P, 2, TOPK], U32), sb("expert_v", [P, 2, TOPK], U32)
        neg_max = sb("neg_max", [P, 1])
        gate_all, gate_sum = sb("gate_all", [P, STEPS, TOPK]), sb("gate_sum", [P, STEPS])
        dots, act, coef = sb("dots", [P, TOPK]), sb("act", [P, TOPK]), sb("coef", [P, TOPK])
        gate_inv = sb("gate_inv", [P, 1])
        ps = ctx.enter_context(nc.psum_tensor("ps", [P, BANKS, 512], F32))
        y_ps = ps[:, 6:8, :]

        x_in, mem_in, small_in = sem("x_in"), sem("mem_in"), sem("small_in")
        gain_in, ln2_in = sem("gain_in"), sem("ln2_in")
        onehot_in, mask_in, chan_in, fourier_in = sem("onehot_in"), sem("mask_in"), sem("chan_in"), sem("fourier_in")
        beta_out, beta_copied, bias_in = sem("beta_out"), sem("beta_copied"), sem("bias_in")
        ring_in = [sem(f"ring_in{j}") for j in range(RING)]
        full = sem("psum_full")
        emptied = {"act": sem("act_emptied"), "dve": sem("dve_emptied")}
        consts = sem("consts")
        h0_ready, h1_ready = sem("h0_ready"), sem("h1_ready")
        nm_ready, exp_ready, prob_ready = sem("nm_ready"), sem("exp_ready"), sem("prob_ready")
        dve_step, dve_passed, pool_passed = sem("dve_step"), sem("dve_passed"), sem("pool_passed")
        u_landed = [sem(f"u_landed{j}") for j in range(ROWS)]
        v_landed = [sem(f"v_landed{j}") for j in range(ROWS)]
        u_used, v_used = sem("u_used"), sem("v_used")
        expert_ready, expert_copied = sem("expert_ready"), sem("expert_copied")
        scores_staged, best_ready, gate_ready = sem("scores_staged"), sem("best_ready"), sem("gate_ready")
        act_ready, coef_ready, diag_ready = sem("act_ready"), sem("coef_ready"), sem("diag_ready")
        y_copied, out_ready, out_stored = sem("y_copied"), sem("out_ready"), sem("out_stored")

        def bank(key, lo=0, hi=512):
            return ps[:, units.bank[key], lo:hi]

        def two_banks(key, lo, hi):
            b = units.bank[key]
            return ps[:, b:b + 2, :].rearrange("p a b -> p (a b)")[:, lo:hi]

        def wait_full(eng, key):
            eng.wait_ge(full, units.index[key] + 1)

        def wait_done(eng, key):
            eng.wait_ge(emptied[units.reader[key]], units.ordinal[key])

        def first(s):
            return isinstance(s, int) and s == 0

        def step_of(t, s):
            return t[:, s, :] if isinstance(s, int) else t[:, bass.ds(s, 1), :].rearrange("p a k -> p (a k)")

        def quads(ap):
            return ap.rearrange("p (a b) -> p a b", a=4)

        block = ctx.enter_context(nc.Block())

        @block.sync
        def _(sp):
            row = lambda a: a.rearrange("(a n) -> a n", a=1).broadcast_to([P, D])
            sp.dma_start(mem_sb, mem[0].rearrange("(m p) d -> p m d", p=P)).then_inc(mem_in, 16)

            def load(i):
                key, _, slot, before, _ = chunks[i]
                what, n = key[0:2]
                if before is not None:
                    wait_full(sp, before)
                dst = slot01[:, slot] if slot < 2 else slot23[:, slot - 2]
                cols = slice(n * CHUNK, (n + 1) * CHUNK)
                w = {"kv": w_mem_kv, "in": w_in, "a": w_a, "b": w_b, "c": w_c, "o": w_o, "pq": w_pq}[what][0]
                sp.dma_start(dst[:, 0:w.shape[0] // P, :], w.rearrange("(k p) n -> p k n", p=P)[:, :, cols]
                             ).then_inc(ring_in[slot], 16)

            load(0)
            for r in range(TILES):
                sp.dma_start(h[:, r, :], x_rows[r]).then_inc(x_in, 16)
            for i in range(1, 5):
                load(i)
            wait_full(sp, ("beta", 5))
            sp.dma_start(cos_t, c_cos.rearrange("(r p) s -> p r s", p=P)).then_inc(fourier_in, 16)
            sp.dma_start(sin_t, c_sin.rearrange("(r p) s -> p r s", p=P)).then_inc(fourier_in, 16)
            for i in range(5, 8):
                load(i)
            sp.wait_ge(beta_out, 16)
            sp.dma_start(beta_copies, beta_dram.unsqueeze(1).broadcast_to([DIL_HEADS * TABLES, P, DELTAS])
                         ).then_inc(beta_copied, 16)
            for i in range(8, 11):
                load(i)
            wait_full(sp, ("Y", 3))
            sp.wait_ge(beta_copied, 16)
            sp.dma_start(bias.rearrange("p h j m -> p (h j) m"),
                         bass.AP(tensor=beta_copies.tensor, offset=P - 1,
                                 ap=[[DELTAS - 1, P], [P * DELTAS, DIL_HEADS * TABLES], [1, P]])
                         ).then_inc(bias_in, 16)
            for i in range(11, len(chunks)):
                load(i)
            sp.wait_ge(h1_ready, TILES)
            sp.dma_start(gains[:, 0, :], row(ln2_g[0])).then_inc(ln2_in, 16)
            sp.dma_start(gains[:, 1, :], row(ln2_b[0])).then_inc(ln2_in, 16)
            for t in range(TILES):
                sp.wait_ge(out_ready, t + 1)
                sp.dma_start(out_rows[t], y_sb).then_inc(out_stored, 16)
            sp.wait_ge(out_stored, 16 * TILES)

        @block.gpsimd
        def _(pool):
            row = lambda a: a.rearrange("(a n) -> a n", a=1)
            pool.dma_start(b_rows, b_in[0].rearrange("(t p) -> t p", p=P)).then_inc(small_in, 16)
            pool.dma_start(keys[:, 0:HD], sub_keys1[0]).then_inc(small_in, 16)
            pool.dma_start(keys[:, HD:2 * HD], sub_keys2[0]).then_inc(small_in, 16)
            pool.dma_start(relb, rel_bias).then_inc(small_in, 16)
            pool.dma_start(onehot, c_onehot).then_inc(onehot_in, 16)
            pool.dma_start(mask, c_mask).then_inc(mask_in, 16)
            pool.dma_start(gains[:, 0, :], row(ln0_g).broadcast_to([P, D])).then_inc(gain_in, 16)
            pool.dma_start(gains[:, 1, :], row(ln0_b).broadcast_to([P, D])).then_inc(gain_in, 16)
            pool.dma_start(chan, c_chan).then_inc(chan_in, 16)
            v_lo = VV[0] * CHUNK
            pool.dma_start(v_bias, row(b_in[0, v_lo:v_lo + 768]).broadcast_to([P, 768])).then_inc(chan_in, 16)
            nc.gpsimd.memset(ident[:], 0.0).then_inc(consts, 1)
            nc.gpsimd.memset(KK[:], 0.0).then_inc(consts, 1)
            nc.gpsimd.iota(iota_u[:], [[1, TOPK]], base=0, channel_multiplier=0).then_inc(consts, 1)
            pool.wait_ge(consts, 3)
            nc.gpsimd.affine_select(out=ident[:], in_=ident[:], compare_op=ALU.not_equal, fill=1.0,
                                    base=0, pattern=[[-1, P]], channel_multiplier=1).then_inc(consts, 1)
            nc.gpsimd.tensor_copy(iota_f[:], iota_u[:]).then_inc(consts, 1)
            wait_done(pool, ("beta", 5))
            pool.dma_start(beta_dram.rearrange("(h j) m -> h (j m)", h=DIL_HEADS), beta).then_inc(beta_out, 16)
            pool.wait_ge(h0_ready, TILES)
            pool.dma_start(gains[:, 0, :], row(ln1_g[0]).broadcast_to([P, D])).then_inc(gain_in, 16)
            pool.dma_start(gains[:, 1, :], row(ln1_b[0]).broadcast_to([P, D])).then_inc(gain_in, 16)

            def gather(ring, slot, table, index, landed):
                nc.gpsimd.indirect_dma_start(
                    out=ring[:, slot, :], out_offset=None, in_=table,
                    in_offset=bass.IndirectOffsetOnAxis(ap=index, axis=0)).then_inc(landed[slot], 16)

            def u_row(s, k, b):
                if not (first(s) and k < ROWS):
                    pool.wait_ge(u_used, s * TOPK + (k - ROWS + 1))
                    pool.sem_inc(pool_passed)
                gather(u_ring, k % ROWS, u_tab[0], expert_u[:, b, k:k + 1], u_landed)

            def v_row(s, k, b):
                if not (first(s) and k < ROWS):
                    pool.wait_ge(v_used, s * TOPK + (k - ROWS + 1))
                    pool.sem_inc(pool_passed)
                gather(v_ring, k % ROWS, v_tab[0], expert_v[:, b, k:k + 1], v_landed)

            def stage(s, buf):
                nc.gpsimd.tensor_copy(buf, step_of(expert_all, s)).then_inc(expert_copied, 1)

            def landed(sems, s):
                for j in range(ROWS):
                    pool.wait_ge(sems[j], s * 32 + 32)
                pool.sem_inc(pool_passed)

            def window(w, b):
                pool.wait_ge(expert_ready, w + 2)
                pool.sem_inc(pool_passed)
                if not first(w):
                    landed(u_landed, w - 1)
                    if not (isinstance(w, int) and w == 1):
                        landed(v_landed, w - 2)
                stage(w + 1, expert_u[:, 1 - b, :])
                stage(w, expert_v[:, b, :])
                pool.wait_ge(expert_copied, w * 2 + 3)
                pool.sem_inc(pool_passed)
                for k in range(TOPK):
                    u_row(w + 1, k, 1 - b)
                    v_row(w, k, b)

            pool.wait_ge(expert_ready, 1)
            stage(0, expert_u[:, 0, :])
            stage(0, expert_v[:, 0, :])
            pool.wait_ge(expert_copied, 2)
            for k in range(TOPK):
                u_row(0, k, 0)
            wait_full(pool, ("Q", 0, 7))
            for k in range(ROWS):
                v_row(0, k, 0)
            pool.wait_ge(expert_ready, 2)
            stage(1, expert_u[:, 1, :])
            pool.wait_ge(expert_copied, 3)
            for k in range(ROWS):
                u_row(1, k, 1)
            for k in range(ROWS, TOPK):
                v_row(0, k, 0)
                u_row(1, k, 1)
            window(1, 1)
            window(2, 0)
            with pool.Fori(0, (STEPS - 4) // 2) as pair:
                window(pair * 2 + 3, 1)
                window(pair * 2 + 4, 0)
            last = STEPS - 1
            landed(v_landed, last - 2)
            stage(last, expert_v[:, 1, :])
            pool.wait_ge(expert_copied, last * 2 + 2)
            for k in range(TOPK):
                v_row(last, k, 1)

        @block.tensor
        def _(pe):
            def begin(key):
                for k in sorted(units.before[key], key=lambda k: units.index[k]):
                    wait_done(pe, k)

            def chunk(key):
                _, _, slot, _, value = chunk_at[key]
                pe.wait_ge(ring_in[slot], value)
                return slot01[:, slot] if slot < 2 else slot23[:, slot - 2]

            def mm(dst, lhsT, rhs, start, stop):
                return nc.tensor.matmul(dst, lhsT, rhs, start=start, stop=stop, skip_group_check=True)

            def product(key, dst, pairs):
                begin(key)
                for n, (lhsT, rhs) in enumerate(pairs):
                    last = mm(dst, lhsT, rhs, n == 0, n == len(pairs) - 1)
                last.then_inc(full, 1)

            def transposes(key, srcs):
                begin(key)
                for n, src in enumerate(srcs):
                    last = nc.tensor.transpose(bank(key, n * P, (n + 1) * P), src, ident[:])
                last.then_inc(full, 1)

            pe.wait_ge(consts, 5)
            pe.wait_ge(mem_in, 16)
            for m in range(2):
                for q in range(2):
                    transposes(("memT", m, q), [mem_sb[:, m, d * P:(d + 1) * P] for d in range(4 * q, 4 * q + 4)])
            for m in range(2):
                for q in range(2):
                    wait_done(pe, ("memT", m, q))
            for n in range(4):
                w = chunk(("kv", n // 2))
                product(("kT", n), bank(("kT", n), 0, MEM),
                        [(w[:, k, (n % 2) * P:(n % 2 + 1) * P], memT[:, k, :]) for k in range(DK)])
            for c in range(2):
                w = chunk(("kv", 2 + c))
                for m in range(2):
                    product(("vm", c, m), bank(("vm", c, m), 0, CHUNK),
                            [(memT[:, k, m * P:(m + 1) * P], w[:, k, :]) for k in range(DK)])
            pe.wait_ge(small_in, 64)
            begin(("bT",))
            nc.tensor.transpose(bank(("bT",), 0, 50), b_rows, ident[0:50, 0:50]).then_inc(full, 1)
            transposes(("KK",), [keys])
            pe.wait_ge(onehot_in, 16)
            for b in range(6):
                lo, hi, g = BETA_CUTS[b], BETA_CUTS[b + 1], BETA_GROUP[b]
                product(("beta", b), bank(("beta", b), 0, hi - lo)[0:DIL_HEADS],
                        [(relb[:, DIL_HEADS * g:DIL_HEADS * (g + 1)], onehot[:, lo:hi])])
            for r in range(TILES):
                pe.wait_ge(h0_ready, r + 1)
                for q in range(2):
                    transposes(("h0T", r, q), [h[:, r, d * P:(d + 1) * P] for d in range(4 * q, 4 * q + 4)])
            wait_done(pe, ("h0T", TILES - 1, 1))

            def project(n):
                w = chunk(("in", n // 2))
                product(("z", n), bank(("z", n)),
                        [(w[:, k, (n % 2) * P:(n % 2 + 1) * P], hT[:, k, :]) for k in range(DK)])

            for n in range(4):
                project(n)
            pe.wait_ge(chan_in, 32)
            wait_done(pe, ("z", 3))
            for r in range(TILES):
                for gg in range(2):
                    key = ("PQ", r, gg)
                    begin(key)
                    for g in range(2):
                        last = mm(bank(key, g * 256, (g + 1) * 256), zaT[:, 2 * gg + g, r * P:(r + 1) * P], chan,
                                  True, True)
                    last.then_inc(full, 1)
            wait_done(pe, ("PQ", TILES - 1, 1))
            pe.wait_ge(fourier_in, 32)
            for g in range(4):
                product(("Y", g), bank(("Y", g)),
                        [x for r in range(TILES) for x in ((pq[:, r, g, 0:P], cos_t[:, r, :]),
                                                           (pq[:, r, g, P:2 * P], sin_t[:, r, :]))])
            for n in range(4, 16):
                project(n)
            for c in range(3):
                w = chunk(("in", VV[0] + c))
                for r in range(TILES):
                    product(("v", c, r), bank(("v", c, r), 0, CHUNK),
                            [(hT[:, k, r * P:(r + 1) * P], w[:, k, :]) for k in range(DK)])
            for n in range(22, 26):
                project(n)
            wait_done(pe, ("z", 25))
            wait_done(pe, ("v", 2, TILES - 1))

            def raw_scores(i):
                r, hd = divmod(i, DIL_HEADS)
                key = ("S", i)
                begin(key)
                rows = slice(HD * (hd % 2), HD * (hd % 2) + HD)
                toks = slice(r * P, (r + 1) * P)
                mm(two_banks(key, 768, 1024), zT[:, 12 + hd, toks], kT[:, hd, :], True, True)
                mm(two_banks(key, 0, 512), zT[rows, hd // 2, toks], zT[rows, 6 + hd // 2, :], True, True)
                for g in (1, 2):
                    last = mm(two_banks(key, 384 + 128 * g, 512 + 128 * g), zT[rows, 2 * g + hd // 2, toks],
                              zT[rows, 6 + 2 * g + hd // 2, toks], True, True)
                last.then_inc(full, 1)

            def attended(i):
                r, hd = divmod(i, DIL_HEADS)
                key = ("O", i)
                begin(key)
                wait_done(pe, ("T0", i))
                wait_done(pe, ("T1", i))
                for j in range(6):
                    tile, g = (j, 0) if j < 4 else (r, j - 3)
                    col = g * 256 + (hd // 2) * P
                    mm(bank(key, 0, P), v_sb[:, tile, col:col + P], probT[:, i % 2, j, :], j == 0, j == 5)
                for m in range(2):
                    last = mm(bank(key, P, 2 * P), vm[:, m, hd * P:(hd + 1) * P], probT[:, i % 2, 6 + m, :],
                              m == 0, m == 1)
                last.then_inc(full, 1)

            raw_scores(0)
            for i in range(PAIRS + 1):
                if i + 1 < PAIRS:
                    raw_scores(i + 1)
                if i >= 1:
                    attended(i - 1)
                if i < PAIRS:
                    pe.wait_ge(prob_ready, i + 1)
                    for t in range(2):
                        transposes((f"T{t}", i), [prob[:, i % 2, c * P:(c + 1) * P] for c in range(4 * t, 4 * t + 4)])

            def tail_unit(key):
                what, g = key[0:2]
                toks = slice(g * GW, (g + 1) * GW)
                if what == "G":
                    j, b = key[2:]
                    w = chunk(("in", GA[0] + 4 * b + j // 2, g))
                    product(key, bank(key, 0, GW), [(w[:, k, (j % 2) * P:(j % 2 + 1) * P], hT[:, k, toks])
                                                    for k in range(DK)])
                elif what == "Yo":
                    j, b = key[2:]
                    w = chunk(("abc"[b], j // 2, g))
                    lo, n = ((0, 4), (4, 2), (6, 4))[b]
                    product(key, bank(key, 0, GW), [(w[:, k, (j % 2) * P:(j % 2 + 1) * P], o[g][:, lo + k, :])
                                                    for k in range(n)])
                elif what == "WO":
                    c, r = key[2:]
                    w = chunk(("o", c, g))
                    if (c, r) == (0, 0):
                        wait_done(pe, ("Yo", g, DK - 1, 2))
                    product(key, bank(key, 0, CHUNK), [(merged[:, k, r * P:(r + 1) * P], w[:, k, :])
                                                       for k in range(DK)])
                elif what == "h1T":
                    r, q = key[2:]
                    tile = g * GT + r
                    pe.wait_ge(h1_ready, tile + 1)
                    transposes(key, [h[:, tile, d * P:(d + 1) * P] for d in range(4 * q, 4 * q + 4)])
                elif what == "Q":
                    n = key[2]
                    w = chunk(("pq", n // 2, g))
                    if n == 0:
                        wait_done(pe, ("h1T", g, GT - 1, 1))
                    product(key, bank(key, 0, GW), [(w[:, k, (n % 2) * P:(n % 2 + 1) * P], hT[:, k, toks])
                                                    for k in range(DK)])
                elif what == "SC":
                    n = key[2]
                    wait_done(pe, ("Q", g, n))
                    begin(key)
                    for r in range(GT):
                        last = mm(bank(key, r * 2 * KEYS, (r + 1) * 2 * KEYS), qT[:, n % 2, r * P:(r + 1) * P],
                                  KK[:], True, True)
                    last.then_inc(full, 1)

            wait_done(pe, ("O", PAIRS - 1))
            gates, wo, h1t, q = tail_units(0)
            for key, _ in gates + sum(wo, []) + h1t + sum(q, []):
                tail_unit(key)

            def weigh(s, k, start):
                pe.wait_ge(diag_ready, s * TOPK + k + 1)
                pe.wait_ge(v_landed[k % ROWS], s * 32 + 16 * (k // ROWS) + 16)
                for half in range(2):
                    last = mm(y_ps[:, half, :], diag[:, k % DIAGS, :], v_ring[:, k % ROWS, half * 512:(half + 1) * 512],
                              start and k == 0, False)
                last.then_inc(v_used, 1)

            for key in units.before["y"]:
                wait_done(pe, key)
            for w in range(2 * HEADS):
                if w == HEADS:
                    pe.wait_ge(y_copied, 1)
                for k in range(TOPK):
                    weigh(w, k, w % HEADS == 0)
                    for key in slots.get((w, k), ()):
                        tail_unit(key)
            with pe.Fori(2, TILES) as t:
                pe.wait_ge(y_copied, t)
                for k in range(TOPK):
                    weigh(t * HEADS, k, True)
                with pe.Fori(1, HEADS) as hd:
                    for k in range(TOPK):
                        weigh(t * HEADS + hd, k, False)

        @block.scalar
        def _(sca):
            done = emptied["act"]

            def take(key, dst, src, func=ACT.Copy, **kw):
                wait_full(sca, key)
                nc.scalar.activation(dst, src, func, **kw).then_inc(done, 1)

            for m in range(2):
                for q in range(2):
                    take(("memT", m, q), memT[:, 4 * q:4 * q + 4, m * P:(m + 1) * P], quads(bank(("memT", m, q))))
            for n in range(4):
                take(("kT", n), kT[:, n, :], bank(("kT", n), 0, MEM))
            for c in range(2):
                for m in range(2):
                    take(("vm", c, m), vm[:, m, c * CHUNK:(c + 1) * CHUNK], bank(("vm", c, m), 0, CHUNK))
            take(("bT",), bT[:], bank(("bT",), 0, 50))
            wait_done(sca, ("bT",))
            wait_done(sca, ("beta", 5))
            for r in range(TILES):
                for q in range(2):
                    take(("h0T", r, q), hT[:, 4 * q:4 * q + 4, r * P:(r + 1) * P], quads(bank(("h0T", r, q))))
            for n in range(4):
                take(("z", n), zaT[:, n, :], bank(("z", n)), ACT.Identity, bias=bT[:, n:n + 1])
            sca.wait_ge(beta_out, 16)
            for g in range(4):
                key = ("Y", g)
                wait_full(sca, key)
                nc.scalar.activation(o[0][:, g, :], bank(key, 0, GW), ACT.Copy)
                nc.scalar.activation(o[1][:, g, :], bank(key, GW, 2 * GW), ACT.Copy).then_inc(done, 1)
            for n in list(range(4, 16)) + list(range(22, 26)):
                place = n - 4 if n < 16 else n - 10
                take(("z", n), zT[:, place, :], bank(("z", n)), ACT.Identity, bias=bT[:, n:n + 1])

            def exps(i):
                sca.wait_ge(nm_ready, i + 1)
                if i >= 2:
                    wait_full(sca, ("T1", i - 2))
                key = ("S", i)
                nc.scalar.activation(prob[:, i % 2, 0:768], prob[:, i % 2, 0:768], ACT.Exp, scale=SCALE_B,
                                     bias=nm[:, i % 2, 0:1], accum_out=sums[:, i % 2, 0:1]).then_inc(exp_ready, 1)
                nc.scalar.activation(prob[:, i % 2, 768:1024], two_banks(key, 768, 1024), ACT.Exp, scale=SCALE_C,
                                     bias=nm[:, i % 2, 1:2], accum_out=sums[:, i % 2, 1:2]).then_inc(done, 1)

            exps(0)
            for i in range(PAIRS):
                if i + 1 < PAIRS:
                    exps(i + 1)
                if i >= 2:
                    wait_full(sca, ("O", i - 2))
                take(("T0", i), probT[:, i % 2, 0:4, :], quads(bank(("T0", i))))

            def tail_unit(key):
                what, g = key[0:2]
                if what == "G":
                    j, b = key[2:]
                    at_n = BRANCH_AT[j, b]
                    if at_n >= SIGS or g >= 1:
                        wait_done(sca, ("Yo", g - (at_n < SIGS)) + BRANCH_ORDER[at_n - SIGS])
                    n = 2 * GA[0] + 8 * b + j
                    take(key, sig[:, at_n % SIGS, :], bank(key, 0, GW), ACT.Sigmoid, bias=bT[:, n:n + 1])
                elif what == "h1T":
                    r, q = key[2:]
                    tile = g * GT + r
                    take(key, hT[:, 4 * q:4 * q + 4, tile * P:(tile + 1) * P], quads(bank(key)))
                elif what == "Q":
                    n = key[2]
                    if n >= 2:
                        wait_full(sca, ("SC", g, n - 2))
                    elif g >= 1:
                        wait_full(sca, ("SC", g - 1, n + 6))
                    take(key, qT[:, n % 2, :], bank(key, 0, GW))

            gates, wo, h1t, q = tail_units(0)
            for key, reader in gates + sum(wo, []) + h1t:
                if reader == "act":
                    tail_unit(key)

            def stage_scores(s, slot):
                nc.scalar.copy(s12, step_of(scores, slot)).then_inc(scores_staged, 1)

            def gates_of(s):
                sca.wait_ge(best_ready, s + 1)
                nc.scalar.activation(step_of(gate_all, s), best[:], ACT.Exp, bias=neg_max[:, 0:1],
                                     accum_out=gate_sum[:, bass.ds(s, 1)]).then_inc(gate_ready, 1)

            def activate(s):
                sca.wait_ge(u_used, s * TOPK + TOPK)
                if not first(s):
                    sca.wait_ge(coef_ready, s)
                nc.scalar.activation(act[:], dots[:], ACT.Gelu).then_inc(act_ready, 1)

            def diagonal(s, k):
                if k == 0:
                    sca.wait_ge(coef_ready, s + 1)
                if not first(s):
                    sca.wait_ge(v_used, s * TOPK + (k - TOPK + 1))
                nc.scalar.activation(diag[:, k, :], ident[:], ACT.Copy, scale=coef[:, k:k + 1]).then_inc(diag_ready, 1)

            def copy_y(t):
                sca.wait_ge(v_used, (t + 1) * HEADS * TOPK)
                if t >= 1:
                    sca.wait_ge(out_stored, 16 * t)
                nc.scalar.copy(y_sb, y_ps.rearrange("p a b -> p (a b)")).then_inc(y_copied, 1)

            def window(w, ahead=True, more=True, units_of=None, offset=0):
                for k in range(TOPK):
                    diagonal(w, k)
                    if k == TOPK // 2 and (ahead or more):
                        gates_of(w + 2)
                    if units_of is not None:
                        for key in slots.get((units_of, k), ()):
                            if units.reader[key] == "act":
                                tail_unit(key)
                if ahead:
                    if units_of == 13:
                        wait_done(sca, ("SC", 1, 7))
                    stage_scores(w + 3, w + 3 - offset)

            for n in range(8):
                tail_unit(("Q", 0, n))
                if n == 0:
                    wait_done(sca, ("SC", 0, 0))
                    stage_scores(0, 0)
                if n == 4:
                    gates_of(0)
                    wait_done(sca, ("SC", 0, 1))
                    stage_scores(1, 1)
            sca.wait_ge(consts, 5)
            wait_done(sca, ("SC", 0, 7))
            gates_of(1)
            activate(0)
            stage_scores(2, 2)
            for w in range(2 * HEADS):
                if w == HEADS:
                    copy_y(0)
                window(w, units_of=w)
                activate(w + 1)
            copy_y(1)
            with sca.Fori(2 * HEADS, 3 * HEADS - 3) as w:
                window(w)
                activate(w + 1)
            for w in range(3 * HEADS - 3, 3 * HEADS):
                window(w, offset=SCORE_SLOTS)
                activate(w + 1)
            copy_y(2)
            with sca.Fori(3 * HEADS, STEPS - 3) as w:
                window(w, offset=SCORE_SLOTS)
                activate(w + 1)
            window(STEPS - 3, ahead=False)
            activate(STEPS - 2)
            window(STEPS - 2, ahead=False, more=False)
            activate(STEPS - 1)
            window(STEPS - 1, ahead=False, more=False)
            copy_y(3)

        @block.vector
        def _(dve):
            done = emptied["dve"]

            class Chain:

                def __init__(self, base):
                    self.base, self.n = base, 0

                def value(self):
                    return self.base + self.n

                def add(self, *ins):
                    for x in ins:
                        x.then_inc(dve_step, 1)
                        self.n += 1

                def wait(self):
                    dve.wait_ge(dve_step, self.value())
                    if not isinstance(self.base, int):
                        dve.sem_inc(dve_passed)

                def link(self, *ins):
                    self.add(*ins)
                    self.wait()

            c = Chain(0)

            def layer_norm(x, tiles, c, landed, value, ready):
                n = len(tiles)
                at_n = slice(tiles[0], tiles[0] + n)
                for m in range(0, n, GT):
                    for i, r in enumerate(tiles[m:m + GT]):
                        c.add(*[nc.vector.bn_stats(stats[:, i, j, :], x(r)[:, j * 512:(j + 1) * 512])
                                for j in range(2)])
                    c.wait()
                    c.link(*[nc.vector.bn_aggr(moments[:, r, :], stats[:, i, :, :].rearrange("p a b -> p (a b)"))
                             for i, r in enumerate(tiles[m:m + GT])])
                c.link(nc.vector.tensor_scalar(rs[:, 0, at_n], moments[:, at_n, 1], EPS, None, ALU.add))
                c.link(nc.vector.tensor_scalar(rs[:, 1, at_n].bitcast(I32), rs[:, 0, at_n].bitcast(I32), 1, None,
                                               ALU.arith_shift_right))
                c.link(nc.vector.tensor_scalar(rs[:, 2, at_n].bitcast(I32), rs[:, 1, at_n].bitcast(I32), -1.0,
                                               RSQRT_GUESS, ALU.mult, ALU.add))
                for _ in range(3):
                    c.link(nc.vector.tensor_tensor(rs[:, 3, at_n], rs[:, 2, at_n], rs[:, 2, at_n], ALU.mult))
                    c.link(nc.vector.tensor_tensor(rs[:, 3, at_n], rs[:, 3, at_n], rs[:, 0, at_n], ALU.mult))
                    c.link(nc.vector.tensor_scalar(rs[:, 4, at_n], rs[:, 3, at_n], -0.5, 1.5, ALU.mult, ALU.add))
                    c.link(nc.vector.tensor_tensor(rs[:, 2, at_n], rs[:, 2, at_n], rs[:, 4, at_n], ALU.mult))
                dve.wait_ge(landed, value)
                for r in tiles:
                    c.link(nc.vector.scalar_tensor_tensor(
                        out=x(r), in0=x(r), scalar=moments[:, r, 0:1], in1=gains[:, 0, :], op0=ALU.subtract,
                        op1=ALU.mult))
                    nc.vector.scalar_tensor_tensor(
                        out=x(r), in0=x(r), scalar=rs[:, 2, r:r + 1], in1=gains[:, 1, :], op0=ALU.mult,
                        op1=ALU.add).then_inc(ready, 1)

            h_tile = lambda r: h[:, r, :]
            dve.wait_ge(x_in, 16 * TILES)
            layer_norm(h_tile, list(range(TILES)), c, gain_in, 32, h0_ready)
            wait_full(dve, ("KK",))
            dve.wait_ge(consts, 5)
            nc.vector.tensor_copy(KK[0:HD, 0:P], bank(("KK",), 0, P)[0:HD])
            nc.vector.tensor_copy(KK[HD:P, P:2 * P], bank(("KK",), 0, P)[HD:P]).then_inc(done, 1)
            dve.wait_ge(mask_in, 16)
            for b in range(6):
                key = ("beta", b)
                wait_full(dve, key)
                lo, hi = BETA_CUTS[b], BETA_CUTS[b + 1]
                nc.vector.scalar_tensor_tensor(out=beta[:, lo:hi], in0=bank(key, 0, hi - lo)[0:DIL_HEADS],
                                               scalar=1.0 / SCALE_B, in1=mask[:, lo:hi], op0=ALU.mult,
                                               op1=ALU.add).then_inc(done, 1)
            for r in range(TILES):
                for gg in range(2):
                    key = ("PQ", r, gg)
                    wait_full(dve, key)
                    nc.vector.tensor_copy(pq[:, r, 2 * gg:2 * gg + 2, :], bank(key).rearrange("p (g c) -> p g c", g=2)
                                          ).then_inc(done, 1)
            dve.wait_ge(chan_in, 32)
            for b in range(3):
                for r in range(TILES):
                    key = ("v", b, r)
                    wait_full(dve, key)
                    nc.vector.tensor_tensor(v_sb[:, r, b * CHUNK:(b + 1) * CHUNK], bank(key, 0, CHUNK),
                                            v_bias[:, b * CHUNK:(b + 1) * CHUNK], ALU.add).then_inc(done, 1)

            def maxima(i):
                key = ("S", i)
                wait_full(dve, key)
                if i >= 2:
                    wait_done(dve, ("S", i - 2))
                    wait_full(dve, ("T1", i - 2))
                r, hd = divmod(i, DIL_HEADS)
                for lo, hi, j, at_mx in ((0, 512, TILES - 1 - r, 0), (512, 768, TABLES - 2, 2)):
                    c.add(nc.vector.tensor_tensor_reduce(
                        prob[:, i % 2, lo:hi], two_banks(key, lo, hi),
                        bias[:, hd, j:j + (hi - lo) // P, :].rearrange("p j m -> p (j m)"), 1.0, LOWEST,
                        ALU.add, ALU.max, mx[:, i % 2, at_mx:at_mx + 1]))
                c.link(nc.vector.tensor_reduce(mx[:, i % 2, 1:2], two_banks(key, 768, 1024), AX.X, ALU.max))
                nc.vector.tensor_scalar(nm[:, i % 2, 0:1], mx[:, i % 2, 0:1], mx[:, i % 2, 2:3], -SCALE_B,
                                        ALU.max, ALU.mult)
                nc.vector.tensor_scalar(nm[:, i % 2, 1:2], mx[:, i % 2, 1:2], -SCALE_C, None, ALU.mult
                                        ).then_inc(nm_ready, 1)

            def normalise(i):
                wait_done(dve, ("S", i))
                dve.wait_ge(exp_ready, i + 1)
                c.link(nc.vector.reciprocal(rinv[:, i % 2, :], sums[:, i % 2, :]))
                nc.vector.tensor_scalar(prob[:, i % 2, 0:768], prob[:, i % 2, 0:768], rinv[:, i % 2, 0:1], None,
                                        ALU.mult)
                nc.vector.tensor_scalar(prob[:, i % 2, 768:1024], prob[:, i % 2, 768:1024], rinv[:, i % 2, 1:2],
                                        None, ALU.mult).then_inc(prob_ready, 1)

            def take_attended(i):
                r, hd = divmod(i, DIL_HEADS)
                key = ("O", i)
                wait_full(dve, key)
                rows = slice(HD * (hd % 2), HD * (hd % 2) + HD)
                cols = slice((r % GT) * P, (r % GT + 1) * P)
                nc.vector.tensor_copy(o[r // GT][rows, 4 + hd // 2, cols], bank(key, 0, P)[rows])
                nc.vector.tensor_copy(o[r // GT][:, 6 + hd, cols], bank(key, P, 2 * P)).then_inc(done, 1)

            dve.wait_ge(beta_out, 16)
            dve.wait_ge(bias_in, 16)
            maxima(0)
            for i in range(PAIRS + 1):
                if i < PAIRS:
                    normalise(i)
                if i + 1 < PAIRS:
                    maxima(i + 1)
                if i >= 1:
                    take_attended(i - 1)
                if i < PAIRS:
                    if i >= 2:
                        wait_full(dve, ("O", i - 2))
                    wait_full(dve, ("T1", i))
                    nc.vector.tensor_copy(probT[:, i % 2, 4:8, :], quads(bank(("T1", i)))).then_inc(done, 1)

            def tail_unit(key, c):
                what, g = key[0:2]
                wait_full(dve, key)
                if what == "Yo":
                    j, b = key[2:]
                    wait_done(dve, ("G", g, j, b))
                    n = BRANCH_AT[j, b]
                    if b == 0:
                        nc.vector.tensor_tensor(merged[:, j, :], sig[:, n % SIGS, :], bank(key, 0, GW), ALU.mult
                                                ).then_inc(done, 1)
                    else:
                        c.link(nc.vector.tensor_tensor(part[:, n % 2, :], sig[:, n % SIGS, :], bank(key, 0, GW),
                                                       ALU.mult))
                        wait_done(dve, ("Yo", g, j, b - 1))
                        nc.vector.tensor_tensor(merged[:, j, :], merged[:, j, :], part[:, n % 2, :], ALU.add
                                                ).then_inc(done, 1)
                elif what == "WO":
                    n, r = key[2:]
                    tile = g * GT + r
                    cols = slice(n * CHUNK, (n + 1) * CHUNK)
                    nc.vector.scalar_tensor_tensor(out=h[:, tile, cols], in0=h[:, tile, cols], scalar=ALPHA,
                                                   in1=bank(key, 0, CHUNK), op0=ALU.mult, op1=ALU.add
                                                   ).then_inc(done, 1)
                elif what == "SC":
                    n = key[2]
                    for r in range(GT):
                        ins = nc.vector.tensor_copy(scores[:, ((g * GT + r) * HEADS + n) % SCORE_SLOTS, :],
                                                    bank(key, r * 2 * KEYS, (r + 1) * 2 * KEYS))
                    ins.then_inc(done, 1)

            def first_norm(g):
                wait_done(dve, ("WO", g, 3, GT - 1))
                layer_norm(h_tile, list(range(g * GT, (g + 1) * GT)), c, gain_in, 64, h1_ready)

            gates, wo, h1t, q = tail_units(0)
            for key, reader in gates + sum(wo, []):
                if reader == "dve":
                    tail_unit(key, c)
            first_norm(0)
            def dot(s, k, tile):
                if k == 0 and not first(s):
                    dve.wait_ge(act_ready, s)
                dve.wait_ge(u_landed[k % ROWS], s * 32 + 16 * (k // ROWS) + 16)
                row = u_ring[:, k % ROWS, :]
                nc.vector.tensor_tensor_reduce(row, row, h[:, tile, :], 1.0, 0.0, ALU.mult, ALU.add,
                                               dots[:, k:k + 1]).then_inc(u_used, 1)

            def held(s):
                if not isinstance(s, int):
                    dve.sem_inc(dve_passed)

            def top_halves(s, c):
                dve.wait_ge(scores_staged, s + 1)
                held(s)
                half = lambda t, x: t[:, x * KEYS:(x + 1) * KEYS]
                for r in range(2):
                    lo, hi = 8 * r, 8 * r + 8
                    src = s12 if r == 0 else s12b
                    c.link(*[nc.vector.max(v12[:, x, lo:hi], half(src, x)) for x in range(2)])
                    c.add(*[nc.vector.max_index(i12[:, x, lo:hi], v12[:, x, lo:hi], half(src, x)) for x in range(2)])
                    if r == 0:
                        c.add(*[nc.vector.match_replace(half(s12b, x), v12[:, x, lo:hi], half(src, x), LOWEST)
                                for x in range(2)])
                    c.wait()

            def top_pairs(s, c):
                c.link(nc.vector.tensor_tensor(cand, v12[:, 0, :].unsqueeze(2).broadcast_to([P, TOPK, TOPK]),
                                               v12[:, 1, :].unsqueeze(1).broadcast_to([P, TOPK, TOPK]), ALU.add))
                if not first(s):
                    dve.wait_ge(gate_ready, s)
                    held(s)
                flat = lambda t: t.rearrange("p a b -> p (a b)")
                for r in range(2):
                    lo, hi = 8 * r, 8 * r + 8
                    src = flat(cand if r == 0 else candb)
                    c.link(nc.vector.max(best[:, lo:hi], src))
                    c.add(nc.vector.max_index(pos[:, lo:hi], best[:, lo:hi], src))
                    if r == 0:
                        c.add(nc.vector.match_replace(flat(candb), best[:, lo:hi], src, LOWEST))
                    c.wait()
                nc.vector.tensor_scalar(neg_max[:], best[:, 0:1], -1.0, None, ALU.mult).then_inc(best_ready, 1)
                c.link(nc.vector.tensor_scalar(ab[:, 0, :], pos[:], 4, None, ALU.logical_shift_right),
                       nc.vector.tensor_scalar(ab[:, 1, :], pos[:], TOPK - 1, None, ALU.bitwise_and))
                c.link(nc.vector.tensor_tensor(
                    pick[:].rearrange("p x k a -> p (x k) a"),
                    ab[:].rearrange("p x k -> p (x k)").unsqueeze(2).broadcast_to([P, 2 * TOPK, TOPK]),
                    iota_f[:].unsqueeze(1).broadcast_to([P, 2 * TOPK, TOPK]), ALU.is_equal))
                c.link(nc.vector.tensor_tensor(
                    pick[:], pick[:], i12[:].unsqueeze(2).broadcast_to([P, 2, TOPK, TOPK]), ALU.mult))
                c.link(nc.vector.tensor_reduce(e12[:], pick[:], AX.X, ALU.add))
                nc.vector.scalar_tensor_tensor(out=step_of(expert_all, s), in0=e12[:, 0, :], scalar=float(KEYS),
                                               in1=e12[:, 1, :], op0=ALU.mult, op1=ALU.add).then_inc(expert_ready, 1)

            def coefficients(s, c):
                dve.wait_ge(gate_ready, s + 1)
                c.link(nc.vector.reciprocal(gate_inv[:], gate_sum[:, bass.ds(s, 1)]))
                dve.wait_ge(act_ready, s + 1)
                if not first(s):
                    dve.wait_ge(diag_ready, s * TOPK)
                nc.vector.scalar_tensor_tensor(out=coef[:], in0=step_of(gate_all, s), scalar=gate_inv[:, 0:1],
                                               in1=act[:], op0=ALU.mult, op1=ALU.mult).then_inc(coef_ready, 1)

            def second_norm(t):
                dve.wait_ge(y_copied, t + 1)
                c.link(nc.vector.scalar_tensor_tensor(out=y_sb, in0=h[:, t, :], scalar=ALPHA, in1=y_sb,
                                                      op0=ALU.mult, op1=ALU.add))
                layer_norm(lambda r: y_sb, [t], c, ln2_in, 32, out_ready)

            def window(w, tile, c, ahead=True, units_of=None):
                for k in range(TOPK):
                    dot(w + 1, k, tile)
                    if units_of is not None:
                        for key in slots.get((units_of, k), ()):
                            if units.reader[key] == "dve":
                                tail_unit(key, c)
                if ahead:
                    top_halves(w + 3, c)
                coefficients(w + 1, c)
                if ahead:
                    top_pairs(w + 3, c)

            def windows(lo, hi, tile):
                probe = 22
                with dve.Fori(lo, hi) as w:
                    body = Chain((w - lo) * probe + c.value())
                    window(w, tile, body)
                    assert body.n == probe
                c.n += (hi - lo) * probe

            for n in range(HEADS):
                tail_unit(("SC", 0, n), c)
                if n == 0:
                    top_halves(0, c)
                if n == 2:
                    top_pairs(0, c)
            for k in range(ROWS):
                dot(0, k, 0)
            wait_done(dve, ("SC", 0, 7))
            top_halves(1, c)
            for k in range(ROWS, TOPK):
                dot(0, k, 0)
            top_pairs(1, c)
            coefficients(0, c)
            top_halves(2, c)
            top_pairs(2, c)
            for w in range(2 * HEADS):
                if w == 10:
                    first_norm(1)
                if w == 14:
                    second_norm(0)
                window(w, (w + 1) // HEADS, c, units_of=w)
            for t in (2, 3):
                lo = t * HEADS
                windows(lo, lo + 2, t)
                second_norm(t - 1)
                if t == 2:
                    windows(lo + 2, lo + HEADS - 1, t)
                    window(lo + HEADS - 1, t + 1, c)
                else:
                    windows(lo + 2, STEPS - 3, t)
            for w in (STEPS - 3, STEPS - 2):
                window(w, TILES - 1, c, ahead=False)
            second_norm(TILES - 1)


def t5_bucket(rel):
    half, exact = BUCKETS // 2, BUCKETS // 4
    n = np.abs(rel)
    nf = np.maximum(n, 1).astype(np.float32)
    large = exact + (np.log(nf / exact) / np.float32(math.log(1024 / exact)) * (half - exact)).astype(np.int32)
    return np.where(rel > 0, half, 0) + np.where(n < exact, n, np.minimum(large, half - 1))


def shape_constants():
    step = np.arange(DELTAS) - (P - 1)
    onehot = np.zeros((BUCKETS, TABLES, DELTAS), np.float32)
    mask = np.zeros((DIL_HEADS, TABLES, DELTAS), np.float32)
    for j in range(TABLES):
        rel = TILES * step
        if j < TABLES - 2:
            rel = rel + (j - (TILES - 1))
            allowed = np.abs(rel) <= 64
        elif j == TABLES - 2:
            allowed = np.abs(step) <= 64
        else:
            allowed = step % 4 == 0
        onehot[t5_bucket(rel), j, np.arange(DELTAS)] = 1.0
        mask[:, j, ~allowed] = -1e30
    token = np.arange(SEQ).reshape(P, TILES).T.reshape(-1)
    angle = 2 * math.pi / SEQ * ((token[:, None] * token[None, :]) % SEQ)
    ch = np.arange(P)
    phi = 2 * math.pi / P * ((ch[:, None] * ch[None, :]) % P)
    norm = 1.0 / math.sqrt(SEQ * P)
    return {
        "c_onehot": onehot.reshape(BUCKETS, -1),
        "c_mask": mask.reshape(DIL_HEADS, -1),
        "c_chan": (np.concatenate([np.cos(phi), np.sin(phi)], 1) * norm).astype(np.float32),
        "c_cos": np.cos(angle).astype(np.float32),
        "c_sin": (-np.sin(angle)).astype(np.float32),
    }


_INS = ["x", "mem", "rel_bias", "ln0_g", "ln0_b", "w_in", "b_in", "w_a", "w_b", "w_c", "w_mem_kv", "w_o",
        "ln1_g", "ln1_b", "w_pq", "sub_keys1", "sub_keys2", "u_tab", "v_tab", "ln2_g", "ln2_b"]


def kernel(**inputs):
    import numpy as _np
    import concourse.bacc as _bacc
    from concourse import mybir as _mybir
    from concourse.bass_utils import run_bass_kernel_spmd as _run

    nc = _bacc.Bacc("TRN2", target_bir_lowering=False, num_devices=1)
    arrays, args = {}, {}
    given = {name: _np.ascontiguousarray(inputs[name]) for name in _INS}
    for name, a in {**given, **shape_constants()}.items():
        arrays[f"in_{name}_dram"] = a
        args[name] = nc.dram_tensor(f"in_{name}_dram", a.shape, _mybir.dt.from_np(a.dtype), kind="ExternalInput").ap()
    args["out"] = nc.dram_tensor("out_0_dram", (1, SEQ, D), F32, kind="ExternalOutput").ap()
    build(nc, **args)
    r = _run(nc, [arrays], core_ids=[0])
    return r.results[0]["out_0_dram"]
```

```python
from contextlib import ExitStack
import math

import numpy as np

import concourse.bass as bass
from concourse import mybir

F32 = mybir.dt.float32
F32R = mybir.dt.float32r
U32 = mybir.dt.uint32
I32 = mybir.dt.int32
ALU = mybir.AluOpType
ACT = mybir.ActivationFunctionType
AX = mybir.AxisListType

P = 128
D = 1024
SEQ = 512
TILES = SEQ // P
EVEN, ODD = SEQ // 2 + 1, SEQ // 2 - 1
GROUPS = 2
GT = TILES // GROUPS
GW = GT * P
DK = D // P
MEM = 256
CHUNK = 256
RING = 4
PEER_RING = 2
BANKS = 8
BUCKETS = 32
DIL_HEADS = 4
HD = 64
DELTAS = 2 * P
TABLES = 2 * TILES - 1 + 2
BETA_CUTS = [0, 512, 1024, 1536, 1792, 2048, 2304]
BETA_GROUP = [0, 0, 0, 0, 1, 2]
SCALE_B = HD ** -0.5
SCALE_C = 128 ** -0.5
ALPHA = 2.0 ** 0.25
EPS = 1e-5
RSQRT_GUESS = float(0x5F3759DF)

HEADS = 8
TOPK = 16
KEYS = 128
STEPS = TILES * HEADS
ROWS = 8
DIAGS = 16
SCORE_SLOTS = 3 * HEADS
LOWEST = -3.0e38

ZA, QK, VV, QC, GA = range(0, 2), range(2, 8), range(8, 11), range(11, 13), range(13, 25)
SPLIT = list(QK) + list(QC)
PARTS = (GT, 1)
PAIRS = TILES * DIL_HEADS


BRANCH_ORDER = [(2 * jj + i, b) for jj in range(DK // 2) for b in range(3) for i in range(2)]
BRANCH_AT = {key: n for n, key in enumerate(BRANCH_ORDER)}
EARLY_WO = 2
SIGS = 4
EARLY_GATES = 2


class Units:

    def __init__(self):
        self.index, self.bank, self.reader, self.ordinal, self.before = {}, {}, {}, {}, {}
        self.emptied = {"act": 0, "dve": 0}
        self.owner = [None] * BANKS
        self.turn, self.turns = 0, BANKS

    def add(self, key, reader, bank=None, width=1):
        if bank is None:
            bank, self.turn = self.turn, (self.turn + 1) % self.turns
        self.before[key] = {self.owner[b] for b in range(bank, bank + width)} - {None}
        for b in range(bank, bank + width):
            self.owner[b] = key
        self.index[key], self.bank[key], self.reader[key] = len(self.index), bank, reader
        self.emptied[reader] += 1
        self.ordinal[key] = self.emptied[reader]


def tail_units(g):
    gates = []
    for n in range(0, len(BRANCH_ORDER), 2):
        two = BRANCH_ORDER[n:n + 2]
        gates += [(("G", g, j, b), "act") for j, b in two] + [(("Yo", g, j, b), "dve") for j, b in two]
    wo = [[(("WO", g, c, r), "dve") for r in range(GT)] for c in range(4)]
    h1t = [[(("h1T", g, r, q), "act") for q in range(2)] for r in range(GT)]
    return gates, wo, h1t


def query_units(g, p):
    q = [[(("Q", g, n, p), "act")] + ([(("SC", g, n - 1, p), "dve")] if n >= 2 else []) for n in range(HEADS)]
    q[0].append((("SC", g, 0, p), "dve"))
    q[-1].append((("SC", g, HEADS - 1, p), "dve"))
    return q


def first_tail():
    gates, wo, h1t = tail_units(0)
    of_tile = [[chunk[r] for chunk in wo] for r in range(GT)]
    q = [query_units(0, p) for p in range(PARTS[0])]
    rest = of_tile[0] + of_tile[1][:EARLY_WO] + h1t[0] + q[0][0] + of_tile[1][EARLY_WO:] + sum(q[0][1:], [])
    rest += h1t[1] + sum(q[1], [])
    return gates, rest


def window_units():
    gates, wo, h1t = tail_units(1)
    q = query_units(1, 0)
    w = {j: gates[6 * j:6 * j + 6] for j in range(DK)}
    w[8], w[9], w[10] = wo[0] + wo[1], wo[2] + wo[3], []
    w[11] = sum(h1t, []) + q[0] + q[1]
    w[12] = q[2] + q[3] + q[4] + q[5]
    w[13] = q[6] + q[7]
    w[14], w[15] = [], []
    return w


def slot_units():
    out = {}
    for w, items in window_units().items():
        for n, (key, _) in enumerate(items):
            out.setdefault((w, 1 + n * 14 // max(len(items), 1)), []).append(key)
    return out


def plan():
    u = Units()
    for m in range(2):
        for q in range(2):
            u.add(("memT", m, q), "act")
    for n in range(4):
        u.add(("kT", n), "act")
    for c in range(2):
        for m in range(2):
            u.add(("vm", c, m), "act")
    u.add(("bT",), "act")
    u.add(("KK",), "dve")
    for b in range(6):
        u.add(("beta", b), "dve")
    for r in range(TILES):
        for q in range(2):
            u.add(("h0T", r, q), "act")
    for n in range(4):
        u.add(("z", n), "act")
    for r in range(TILES):
        for g in range(2):
            u.add(("PQ", r, g), "dve")
    for g in range(4):
        u.add(("Y", g), "dve")
    for n in range(4, 16):
        u.add(("z", n), "act")
    for n in range(22, 26):
        u.add(("z", n), "act")
    u.add(("S", 0), "act", bank=0, width=2)
    u.turn = 2
    for c in range(3):
        for r in range(TILES):
            u.add(("v", c, r), "dve")
    gates, rest = first_tail()
    for i in range(PAIRS + 1):
        if i + 1 < PAIRS:
            u.add(("S", i + 1), "act", bank=2 * ((i + 1) % 2), width=2)
        if i == PAIRS:
            for n, (key, reader) in enumerate(gates[:EARLY_GATES]):
                u.add(key, reader, bank=n)
        if i >= 1:
            u.add(("O", i - 1), "dve", bank=6 + i % 2)
        if i < PAIRS:
            u.add(("T0", i), "act", bank=4)
            u.add(("T1", i), "dve", bank=5)
    u.turn = EARLY_GATES
    for key, reader in gates[EARLY_GATES:] + rest:
        u.add(key, reader)
    u.before["y"] = {u.owner[6], u.owner[7]}
    u.turn, u.turns = 0, 6
    for w in sorted(window_units()):
        for key, reader in window_units()[w]:
            u.add(key, reader)
    return u


def chunk_plan():
    c = []
    for n in range(4):
        c.append((("kv", n), ("kT", 2 * n + 1) if n < 2 else ("vm", n - 2, 1)))
    for n in list(ZA) + list(QK):
        c.append((("in", n), ("z", 2 * n + 1)))
    for n in QC:
        c.append((("in", n), ("z", 2 * n + 1)))
    for n in VV:
        c.append((("in", n), ("v", n - VV[0], TILES - 1)))
    for g in range(GROUPS):
        for jj in range(4):
            for b in range(3):
                c.append((("in", GA[0] + 4 * b + jj, g), ("G", g, 2 * jj + 1, b)))
                c.append((("abc"[b], jj, g), ("Yo", g, 2 * jj + 1, b)))
        for n in range(4):
            c.append((("o", n, g), ("WO", g, n, GT - 1)))
        for n in range(4):
            c.append((("pq", n, g), ("Q", g, 2 * n + 1, PARTS[g] - 1)))
    first_peer = next(i for i, (key, _) in enumerate(c) if key == ("in", GA[0], 1))
    out, held, loads = [], {}, {}
    for i, (key, last) in enumerate(c):
        slot = i % RING if i < first_peer else (i - first_peer) % PEER_RING
        loads[slot] = loads.get(slot, 0) + 1
        out.append((key, last, slot, held.get(slot), 16 * loads[slot]))
        held[slot] = last
    return out


def build(nc, x, mem, rel_bias, ln0_g, ln0_b, w_in, b_in, w_a, w_b, w_c, w_mem_kv, w_o,
          ln1_g, ln1_b, w_pq, sub_keys1, sub_keys2, u_tab, v_tab, ln2_g, ln2_b,
          c_onehot, c_mask, c_chan, c_cos, c_sin, out):
    beta_dram = nc.dram_tensor("beta_rows", [DIL_HEADS * TABLES, DELTAS], F32).ap()
    beta_copies = nc.dram_tensor("beta_copies", [DIL_HEADS * TABLES, P, DELTAS], F32).ap()
    tile_rows = lambda t: t[0].rearrange("(m r) d -> r m d", r=TILES)
    x_rows, out_rows = tile_rows(x), tile_rows(out)
    units, chunks = plan(), chunk_plan()
    chunk_at = {c[0]: c for c in chunks}
    slots = slot_units()
    ctx = ExitStack()
    with ctx:
        def sb(name, shape, dt=F32):
            return ctx.enter_context(nc.sbuf_tensor(name, shape, dt))

        def sem(name):
            return ctx.enter_context(nc.semaphore(name))

        K = 256

        def parts_at(name, kb, size, k):
            with nc.sbuf_tensor(f"below_{name}", [P, kb * K], F32), nc.sbuf_tensor(name, [P, size * K], F32R) as t:
                return t[:].rearrange("p (k n) -> p k n", k=k)

        hT_high = [parts_at(f"hT_high{kb}", kb, 8, 4) for kb in (32, 178)]
        hT_low = parts_at("hT_low", 90, 16, DK)
        w_high = [[parts_at(f"w_high{kb}", kb, 4, 4) for kb in halves]
                  for halves in ((66, 70), (130, 134), (84, 146), (60, 156))]
        w_low = [parts_at(f"w_low{slot}", kb, 8, DK) for slot, kb in enumerate((40, 48, 162, 170))]
        arena = sb("arena", [P, 186 * K])

        def at(kb, size):
            return arena[:, kb * K:(kb + size) * K]

        h = at(0, 16).rearrange("p (r d) -> p r d", r=TILES)
        hT = at(16, 16).rearrange("p (k s) -> p k s", k=DK)
        gains = at(32, 8).rearrange("p (a d) -> p a d", a=2)
        slot01 = at(40, 16).rearrange("p (s k n) -> p s k n", s=2, k=DK)
        o_1 = at(56, 10).rearrange("p (k s) -> p k s", k=10)
        merged = at(66, 8).rearrange("p (k s) -> p k s", k=DK)
        sig = at(74, 4).rearrange("p (b s) -> p b s", b=SIGS)
        part = at(78, 2).rearrange("p (b s) -> p b s", b=2)
        qT = at(80, 2).rearrange("p (b s) -> p b s", b=2)
        scores = at(82, 24).rearrange("p (s k) -> p s k", s=SCORE_SLOTS)
        u_ring = at(106, 32).rearrange("p (j d) -> p j d", j=ROWS)
        v_ring = at(138, 32).rearrange("p (j d) -> p j d", j=ROWS)
        diag = at(170, 8).rearrange("p (j q) -> p j q", j=DIAGS)
        slot23 = at(162, 16).rearrange("p (s k n) -> p s k n", s=2, k=DK)
        o_0 = at(152, 10).rearrange("p (k s) -> p k s", k=10)
        zT = at(106, 32).rearrange("p (t s) -> p t s", t=16)
        kT = at(138, 4).rearrange("p (t s) -> p t s", t=4)
        vm = at(142, 4).rearrange("p (m n) -> p m n", m=2)
        v_sb = at(94, 12).rearrange("p (r n) -> p r n", r=TILES)
        B0 = DIL_HEADS * TABLES * P
        bias = arena[:, 66 * K:66 * K + B0].rearrange("p (h j m) -> p h j m", h=DIL_HEADS, j=TABLES)
        prob = at(84, 8).rearrange("p (b k) -> p b k", b=2)
        probT = at(178, 8).rearrange("p (b j q) -> p b j q", b=2, j=8)
        zaT = at(66, 8).rearrange("p (g s) -> p g s", g=4)
        pq = at(74, 16).rearrange("p (r g c) -> p r g c", r=TILES, g=4)
        cos_t = arena[:, 106 * K:106 * K + TILES * EVEN].rearrange("p (r n) -> p r n", r=TILES)
        sin_t = arena[:, 111 * K:111 * K + TILES * ODD].rearrange("p (r n) -> p r n", r=TILES)
        memT = zT[:, 8:12, :].rearrange("p a (b m) -> p (a b) m", m=MEM)
        mem_sb = zT[:, 12:16, :].rearrange("p (m a) b -> p m (a b)", m=2)
        onehot = zT[0:BUCKETS, 0:5, :].rearrange("p a b -> p (a b)")[:, 0:TABLES * DELTAS]
        mask = hT[0:DIL_HEADS, 0:5, :].rearrange("p a b -> p (a b)")[:, 0:TABLES * DELTAS]
        beta = o_1[0:DIL_HEADS, :, :].rearrange("p a b -> p (a b)")[:, 0:TABLES * DELTAS]
        o = [o_0, o_1]
        y_sb = at(178, 4)

        ident = sb("ident", [P, P])
        KK = sb("KK", [P, 2 * P])
        bT = sb("bT", [P, 50])
        early = sb("early", [P, 768 + 256 + 128 + 128 + 12])
        v_bias, chan = early[:, 0:768], early[:, 768:1024]
        keys, b_rows = early[:, 1024:1152], early[0:50, 1152:1280]
        relb = early[0:BUCKETS, 1280:1292]
        stats = sb("stats", [P, GT, 2, 6])
        moments = sb("moments", [P, TILES, 2])
        rs = sb("rs", [P, 5, TILES])
        mx, nm = sb("mx", [P, 2, 3]), sb("nm", [P, 2, 2])
        sums, rinv = sb("sums", [P, 2, 2]), sb("rinv", [P, 2, 2])

        s12 = early[:, 0:256]
        s12b = early[:, 256:512]
        cand = early[:, 512:768].rearrange("p (a b) -> p a b", a=TOPK)
        candb = early[:, 768:1024].rearrange("p (a b) -> p a b", a=TOPK)
        pick = sb("pick", [P, 2, TOPK, TOPK])
        v12, i12 = sb("v12", [P, 2, TOPK]), sb("i12", [P, 2, TOPK], U32)
        best, pos = sb("best", [P, TOPK]), sb("pos", [P, TOPK], U32)
        ab = sb("ab", [P, 2, TOPK], U32)
        iota_f, iota_u = sb("iota_f", [P, TOPK]), sb("iota_u", [P, TOPK], U32)
        e12 = sb("e12", [P, 2, TOPK])
        expert_all = sb("expert_all", [P, STEPS, TOPK], U32)
        expert_u, expert_v = sb("expert_u", [P, 2, TOPK], U32), sb("expert_v", [P, 2, TOPK], U32)
        neg_max = sb("neg_max", [P, 1])
        gate_all, gate_sum = sb("gate_all", [P, STEPS, TOPK]), sb("gate_sum", [P, STEPS])
        dots, act, coef = sb("dots", [P, TOPK]), sb("act", [P, TOPK]), sb("coef", [P, TOPK])
        gate_inv = sb("gate_inv", [P, 1])
        ps = ctx.enter_context(nc.psum_tensor("ps", [P, BANKS, 512], F32))
        y_ps = ps[:, 6:8, :]

        x_in, mem_in, small_in = sem("x_in"), sem("mem_in"), sem("small_in")
        gain_in, ln2_in = sem("gain_in"), sem("ln2_in")
        onehot_in, mask_in, chan_in, fourier_in = sem("onehot_in"), sem("mask_in"), sem("chan_in"), sem("fourier_in")
        beta_out, beta_copied, bias_in = sem("beta_out"), sem("beta_copied"), sem("bias_in")
        ring_in = [sem(f"ring_in{j}") for j in range(RING)]
        full = sem("psum_full")
        emptied = {"act": sem("act_emptied"), "dve": sem("dve_emptied")}
        consts = sem("consts")
        split_ready = sem("split_ready")
        h0_ready, h1_ready = sem("h0_ready"), sem("h1_ready")
        nm_ready, exp_ready, prob_ready = sem("nm_ready"), sem("exp_ready"), sem("prob_ready")
        dve_step, dve_passed, pool_passed = sem("dve_step"), sem("dve_passed"), sem("pool_passed")
        u_landed = [sem(f"u_landed{j}") for j in range(ROWS)]
        v_landed = [sem(f"v_landed{j}") for j in range(ROWS)]
        u_used, v_used = sem("u_used"), sem("v_used")
        expert_ready, expert_copied = sem("expert_ready"), sem("expert_copied")
        scores_staged, best_ready, gate_ready = sem("scores_staged"), sem("best_ready"), sem("gate_ready")
        act_ready, coef_ready, diag_ready = sem("act_ready"), sem("coef_ready"), sem("diag_ready")
        y_copied, out_ready, out_stored = sem("y_copied"), sem("out_ready"), sem("out_stored")

        def bank(key, lo=0, hi=512):
            return ps[:, units.bank[key], lo:hi]

        def two_banks(key, lo, hi):
            b = units.bank[key]
            return ps[:, b:b + 2, :].rearrange("p a b -> p (a b)")[:, lo:hi]

        def wait_full(eng, key):
            eng.wait_ge(full, units.index[key] + 1)

        def wait_done(eng, key):
            eng.wait_ge(emptied[units.reader[key]], units.ordinal[key])

        def first(s):
            return isinstance(s, int) and s == 0

        def step_of(t, s):
            return t[:, s, :] if isinstance(s, int) else t[:, bass.ds(s, 1), :].rearrange("p a k -> p (a k)")

        def query_place(g, n, p):
            tiles = GT // PARTS[g]
            turn = p * HEADS + n
            return g * GT + p * tiles, tiles, turn, qT[:, turn % 2, 0:tiles * P]

        def query_unit_at(g, turn):
            return g, turn % HEADS, turn // HEADS

        def split_chunk(n):
            slot = chunk_at["in", n][2]
            m = SPLIT.index(n)
            high = w_high[m % 2 if n in QK else m - len(QK) + 2]
            return high, slot01[:, slot] if slot < 2 else slot23[:, slot - 2], w_low[slot]

        def quads(ap):
            return ap.rearrange("p (a b) -> p a b", a=4)

        block = ctx.enter_context(nc.Block())

        @block.sync
        def _(sp):
            row = lambda a: a.rearrange("(a n) -> a n", a=1).broadcast_to([P, D])
            sp.dma_start(mem_sb, mem[0].rearrange("(m p) d -> p m d", p=P)).then_inc(mem_in, 16)

            def load(i):
                key, _, slot, before, _ = chunks[i]
                what, n = key[0:2]
                if before is not None:
                    wait_full(sp, before)
                dst = slot01[:, slot] if slot < 2 else slot23[:, slot - 2]
                cols = slice(n * CHUNK, (n + 1) * CHUNK)
                w = {"kv": w_mem_kv, "in": w_in, "a": w_a, "b": w_b, "c": w_c, "o": w_o, "pq": w_pq}[what][0]
                sp.dma_start(dst[:, 0:w.shape[0] // P, :], w.rearrange("(k p) n -> p k n", p=P)[:, :, cols]
                             ).then_inc(ring_in[slot], 16)

            load(0)
            for r in range(TILES):
                sp.dma_start(h[:, r, :], x_rows[r]).then_inc(x_in, 16)
            for i in range(1, 5):
                load(i)
            wait_full(sp, ("beta", 5))
            sp.dma_start(cos_t, c_cos.rearrange("(r p) s -> p r s", p=P)).then_inc(fourier_in, 16)
            sp.dma_start(sin_t, c_sin.rearrange("(r p) s -> p r s", p=P)).then_inc(fourier_in, 16)
            for i in range(5, 8):
                load(i)
            sp.wait_ge(beta_out, 16)
            sp.dma_start(beta_copies, beta_dram.unsqueeze(1).broadcast_to([DIL_HEADS * TABLES, P, DELTAS])
                         ).then_inc(beta_copied, 16)
            before_bias = 4 + len(ZA) + len(QK) + RING - 1
            for i in range(8, before_bias):
                load(i)
            wait_full(sp, ("z", 2 * QK[-1] + 1))
            sp.wait_ge(beta_copied, 16)
            sp.dma_start(bias.rearrange("p h j m -> p (h j) m"),
                         bass.AP(tensor=beta_copies.tensor, offset=P - 1,
                                 ap=[[DELTAS - 1, P], [P * DELTAS, DIL_HEADS * TABLES], [1, P]])
                         ).then_inc(bias_in, 16)
            for i in range(before_bias, len(chunks)):
                load(i)
            sp.wait_ge(h1_ready, TILES)
            sp.dma_start(gains[:, 0, :], row(ln2_g[0])).then_inc(ln2_in, 16)
            sp.dma_start(gains[:, 1, :], row(ln2_b[0])).then_inc(ln2_in, 16)
            for t in range(TILES):
                sp.wait_ge(out_ready, t + 1)
                sp.dma_start(out_rows[t], y_sb).then_inc(out_stored, 16)
            sp.wait_ge(out_stored, 16 * TILES)

        @block.gpsimd
        def _(pool):
            nc.gpsimd.memset(ident[:], 0.0).then_inc(consts, 1)
            nc.gpsimd.memset(KK[:], 0.0).then_inc(consts, 1)
            nc.gpsimd.iota(iota_u[:], [[1, TOPK]], base=0, channel_multiplier=0).then_inc(consts, 1)
            pool.wait_ge(consts, 3)
            nc.gpsimd.affine_select(out=ident[:], in_=ident[:], compare_op=ALU.not_equal, fill=1.0,
                                    base=0, pattern=[[-1, P]], channel_multiplier=1).then_inc(consts, 1)
            nc.gpsimd.tensor_copy(iota_f[:], iota_u[:]).then_inc(consts, 1)
            row = lambda a: a.rearrange("(a n) -> a n", a=1)
            pool.dma_start(b_rows, b_in[0].rearrange("(t p) -> t p", p=P)).then_inc(small_in, 16)
            pool.dma_start(keys[:, 0:HD], sub_keys1[0]).then_inc(small_in, 16)
            pool.dma_start(keys[:, HD:2 * HD], sub_keys2[0]).then_inc(small_in, 16)
            pool.dma_start(relb, rel_bias).then_inc(small_in, 16)
            pool.dma_start(onehot, c_onehot).then_inc(onehot_in, 16)
            pool.dma_start(mask, c_mask).then_inc(mask_in, 16)
            pool.dma_start(gains[:, 0, :], row(ln0_g).broadcast_to([P, D])).then_inc(gain_in, 16)
            pool.dma_start(gains[:, 1, :], row(ln0_b).broadcast_to([P, D])).then_inc(gain_in, 16)
            pool.dma_start(chan, c_chan).then_inc(chan_in, 16)
            v_lo = VV[0] * CHUNK
            pool.dma_start(v_bias, row(b_in[0, v_lo:v_lo + 768]).broadcast_to([P, 768])).then_inc(chan_in, 16)
            wait_done(pool, ("beta", 5))
            pool.dma_start(beta_dram.rearrange("(h j) m -> h (j m)", h=DIL_HEADS), beta).then_inc(beta_out, 16)
            wait_full(pool, ("z", 2 * SPLIT[-1] + 1))
            pool.dma_start(gains[:, 0, :], row(ln1_g[0]).broadcast_to([P, D])).then_inc(gain_in, 16)
            pool.dma_start(gains[:, 1, :], row(ln1_b[0]).broadcast_to([P, D])).then_inc(gain_in, 16)

            def gather(ring, slot, table, index, landed):
                nc.gpsimd.indirect_dma_start(
                    out=ring[:, slot, :], out_offset=None, in_=table,
                    in_offset=bass.IndirectOffsetOnAxis(ap=index, axis=0)).then_inc(landed[slot], 16)

            def u_row(s, k, b):
                if not (first(s) and k < ROWS):
                    pool.wait_ge(u_used, s * TOPK + (k - ROWS + 1))
                    pool.sem_inc(pool_passed)
                gather(u_ring, k % ROWS, u_tab[0], expert_u[:, b, k:k + 1], u_landed)

            def v_row(s, k, b):
                if not (first(s) and k < ROWS):
                    pool.wait_ge(v_used, s * TOPK + (k - ROWS + 1))
                    pool.sem_inc(pool_passed)
                gather(v_ring, k % ROWS, v_tab[0], expert_v[:, b, k:k + 1], v_landed)

            def stage(s, buf):
                nc.gpsimd.tensor_copy(buf, step_of(expert_all, s)).then_inc(expert_copied, 1)

            def landed(sems, s):
                for j in range(ROWS):
                    pool.wait_ge(sems[j], s * 32 + 32)
                pool.sem_inc(pool_passed)

            def window(w, b):
                pool.wait_ge(expert_ready, w + 2)
                pool.sem_inc(pool_passed)
                if not first(w):
                    landed(u_landed, w - 1)
                    if not (isinstance(w, int) and w == 1):
                        landed(v_landed, w - 2)
                stage(w + 1, expert_u[:, 1 - b, :])
                stage(w, expert_v[:, b, :])
                pool.wait_ge(expert_copied, w * 2 + 3)
                pool.sem_inc(pool_passed)
                for k in range(TOPK):
                    u_row(w + 1, k, 1 - b)
                    v_row(w, k, b)

            pool.wait_ge(expert_ready, 1)
            stage(0, expert_u[:, 0, :])
            stage(0, expert_v[:, 0, :])
            pool.wait_ge(expert_copied, 2)
            for k in range(TOPK):
                u_row(0, k, 0)
            for k in range(ROWS - 2):
                v_row(0, k, 0)
            pool.wait_ge(expert_ready, 2)
            stage(1, expert_u[:, 1, :])
            pool.wait_ge(expert_copied, 3)
            for k in range(ROWS):
                u_row(1, k, 1)
            wait_full(pool, ("Q", 0, HEADS - 1, PARTS[0] - 1))
            for k in (ROWS - 2, ROWS - 1):
                v_row(0, k, 0)
            for k in range(ROWS, TOPK):
                v_row(0, k, 0)
                u_row(1, k, 1)
            window(1, 1)
            window(2, 0)
            with pool.Fori(0, (STEPS - 4) // 2) as pair:
                window(pair * 2 + 3, 1)
                window(pair * 2 + 4, 0)
            last = STEPS - 1
            landed(v_landed, last - 2)
            stage(last, expert_v[:, 1, :])
            pool.wait_ge(expert_copied, last * 2 + 2)
            for k in range(TOPK):
                v_row(last, k, 1)

        @block.tensor
        def _(pe):
            def begin(key):
                for k in sorted(units.before[key], key=lambda k: units.index[k]):
                    wait_done(pe, k)

            def chunk(key):
                _, _, slot, _, value = chunk_at[key]
                pe.wait_ge(ring_in[slot], value)
                return slot01[:, slot] if slot < 2 else slot23[:, slot - 2]

            def mm(dst, lhsT, rhs, start, stop):
                return nc.tensor.matmul(dst, lhsT, rhs, start=start, stop=stop, skip_group_check=True)

            def product(key, dst, pairs):
                begin(key)
                for n, (lhsT, rhs) in enumerate(pairs):
                    last = mm(dst, lhsT, rhs, n == 0, n == len(pairs) - 1)
                last.then_inc(full, 1)

            def transposes(key, srcs):
                begin(key)
                for n, src in enumerate(srcs):
                    last = nc.tensor.transpose(bank(key, n * P, (n + 1) * P), src, ident[:])
                last.then_inc(full, 1)

            pe.wait_ge(consts, 5)
            pe.wait_ge(mem_in, 16)
            for m in range(2):
                for q in range(2):
                    transposes(("memT", m, q), [mem_sb[:, m, d * P:(d + 1) * P] for d in range(4 * q, 4 * q + 4)])
            for m in range(2):
                for q in range(2):
                    wait_done(pe, ("memT", m, q))
            for n in range(4):
                w = chunk(("kv", n // 2))
                product(("kT", n), bank(("kT", n), 0, MEM),
                        [(w[:, k, (n % 2) * P:(n % 2 + 1) * P], memT[:, k, :]) for k in range(DK)])
            for c in range(2):
                w = chunk(("kv", 2 + c))
                for m in range(2):
                    product(("vm", c, m), bank(("vm", c, m), 0, CHUNK),
                            [(memT[:, k, m * P:(m + 1) * P], w[:, k, :]) for k in range(DK)])
            pe.wait_ge(small_in, 64)
            begin(("bT",))
            nc.tensor.transpose(bank(("bT",), 0, 50), b_rows, ident[0:50, 0:50]).then_inc(full, 1)
            transposes(("KK",), [keys])
            pe.wait_ge(onehot_in, 16)
            for b in range(6):
                lo, hi, g = BETA_CUTS[b], BETA_CUTS[b + 1], BETA_GROUP[b]
                product(("beta", b), bank(("beta", b), 0, hi - lo)[0:DIL_HEADS],
                        [(relb[:, DIL_HEADS * g:DIL_HEADS * (g + 1)], onehot[:, lo:hi])])
            for r in range(TILES):
                pe.wait_ge(h0_ready, r + 1)
                for q in range(2):
                    transposes(("h0T", r, q), [h[:, r, d * P:(d + 1) * P] for d in range(4 * q, 4 * q + 4)])
            wait_done(pe, ("h0T", TILES - 1, 1))

            def project(n):
                w = chunk(("in", n // 2))
                product(("z", n), bank(("z", n)),
                        [(w[:, k, (n % 2) * P:(n % 2 + 1) * P], hT[:, k, :]) for k in range(DK)])

            for n in range(4):
                project(n)
            pe.wait_ge(chan_in, 32)
            wait_done(pe, ("z", 3))
            for r in range(TILES):
                for gg in range(2):
                    key = ("PQ", r, gg)
                    begin(key)
                    for g in range(2):
                        last = mm(bank(key, g * 256, (g + 1) * 256), zaT[:, 2 * gg + g, r * P:(r + 1) * P], chan,
                                  True, True)
                    last.then_inc(full, 1)
            wait_done(pe, ("PQ", TILES - 1, 1))
            pe.wait_ge(fourier_in, 32)
            for g in range(4):
                key = ("Y", g)
                begin(key)
                for lo, table, part_of in ((0, cos_t, pq[:, :, g, 0:P]), (EVEN, sin_t, pq[:, :, g, P:2 * P])):
                    for r in range(TILES):
                        last = mm(bank(key, lo, lo + table.shape[2]), part_of[:, r, :], table[:, r, :],
                                  r == 0, r == TILES - 1)
                last.then_inc(full, 1)
            def project_split(n):
                pe.wait_ge(split_ready, 2 * (1 + SPLIT.index(n // 2) + 1))
                high, _, low = split_chunk(n // 2)
                cols = slice((n % 2) * P, (n % 2 + 1) * P)
                product(("z", n), bank(("z", n)),
                        [(w[:, cols], x) for k in range(DK)
                         for w, x in ((high[k // 4][:, k % 4, :], hT_low[:, k, :]),
                                      (high[k // 4][:, k % 4, :], hT_high[k // 4][:, k % 4, :]),
                                      (low[:, k, :], hT_high[k // 4][:, k % 4, :]))])

            for n in list(range(4, 16)) + list(range(22, 26)):
                project_split(n)
            wait_done(pe, ("z", 25))

            def raw_scores(i):
                r, hd = divmod(i, DIL_HEADS)
                key = ("S", i)
                begin(key)
                rows = slice(HD * (hd % 2), HD * (hd % 2) + HD)
                toks = slice(r * P, (r + 1) * P)
                mm(two_banks(key, 768, 1024), zT[:, 12 + hd, toks], kT[:, hd, :], True, True)
                mm(two_banks(key, 0, 512), zT[rows, hd // 2, toks], zT[rows, 6 + hd // 2, :], True, True)
                for g in (1, 2):
                    last = mm(two_banks(key, 384 + 128 * g, 512 + 128 * g), zT[rows, 2 * g + hd // 2, toks],
                              zT[rows, 6 + 2 * g + hd // 2, toks], True, True)
                last.then_inc(full, 1)

            def attended(i):
                r, hd = divmod(i, DIL_HEADS)
                key = ("O", i)
                begin(key)
                wait_done(pe, ("T0", i))
                wait_done(pe, ("T1", i))
                for j in range(6):
                    tile, g = (j, 0) if j < 4 else (r, j - 3)
                    col = g * 256 + (hd // 2) * P
                    mm(bank(key, 0, P), v_sb[:, tile, col:col + P], probT[:, i % 2, j, :], j == 0, j == 5)
                for m in range(2):
                    last = mm(bank(key, P, 2 * P), vm[:, m, hd * P:(hd + 1) * P], probT[:, i % 2, 6 + m, :],
                              m == 0, m == 1)
                last.then_inc(full, 1)

            def tail_unit(key):
                what, g = key[0:2]
                toks = slice(g * GW, (g + 1) * GW)
                if what == "G":
                    j, b = key[2:]
                    w = chunk(("in", GA[0] + 4 * b + j // 2, g))
                    product(key, bank(key, 0, GW), [(w[:, k, (j % 2) * P:(j % 2 + 1) * P], hT[:, k, toks])
                                                    for k in range(DK)])
                elif what == "Yo":
                    j, b = key[2:]
                    w = chunk(("abc"[b], j // 2, g))
                    lo, n = ((0, 4), (4, 2), (6, 4))[b]
                    product(key, bank(key, 0, GW), [(w[:, k, (j % 2) * P:(j % 2 + 1) * P], o[g][:, lo + k, :])
                                                    for k in range(n)])
                elif what == "WO":
                    c, r = key[2:]
                    w = chunk(("o", c, g))
                    if (c, r) == (0, 0):
                        wait_done(pe, ("Yo", g, DK - 1, 2))
                    product(key, bank(key, 0, CHUNK), [(merged[:, k, r * P:(r + 1) * P], w[:, k, :])
                                                       for k in range(DK)])
                elif what == "h1T":
                    r, q = key[2:]
                    tile = g * GT + r
                    pe.wait_ge(h1_ready, tile + 1)
                    transposes(key, [h[:, tile, d * P:(d + 1) * P] for d in range(4 * q, 4 * q + 4)])
                elif what == "Q":
                    n = key[2]
                    w = chunk(("pq", n // 2, g))
                    tile, tiles, _, _ = query_place(*key[1:])
                    if n == 0:
                        wait_done(pe, ("h1T", g, tile + tiles - 1 - g * GT, 1))
                    product(key, bank(key, 0, tiles * P), [(w[:, k, (n % 2) * P:(n % 2 + 1) * P],
                                                            hT[:, k, tile * P:(tile + tiles) * P])
                                                           for k in range(DK)])
                elif what == "SC":
                    _, tiles, _, query = query_place(*key[1:])
                    wait_done(pe, ("Q",) + key[1:])
                    begin(key)
                    for r in range(tiles):
                        last = mm(bank(key, r * 2 * KEYS, (r + 1) * 2 * KEYS), query[:, r * P:(r + 1) * P],
                                  KK[:], True, True)
                    last.then_inc(full, 1)

            raw_scores(0)
            for c in range(3):
                w = chunk(("in", VV[0] + c))
                for r in range(TILES):
                    product(("v", c, r), bank(("v", c, r), 0, CHUNK),
                            [(hT[:, k, r * P:(r + 1) * P], w[:, k, :]) for k in range(DK)])
            wait_done(pe, ("v", 2, TILES - 1))
            gates, rest = first_tail()
            for i in range(PAIRS + 1):
                if i + 1 < PAIRS:
                    raw_scores(i + 1)
                if i == PAIRS:
                    for key, _ in gates[:EARLY_GATES]:
                        tail_unit(key)
                if i >= 1:
                    attended(i - 1)
                if i < PAIRS:
                    pe.wait_ge(prob_ready, i + 1)
                    for t in range(2):
                        transposes((f"T{t}", i), [prob[:, i % 2, c * P:(c + 1) * P] for c in range(4 * t, 4 * t + 4)])

            wait_done(pe, ("O", PAIRS - 1))
            for key, _ in gates[EARLY_GATES:] + rest:
                tail_unit(key)

            def weigh(s, k, start):
                pe.wait_ge(diag_ready, s * TOPK + k + 1)
                pe.wait_ge(v_landed[k % ROWS], s * 32 + 16 * (k // ROWS) + 16)
                for half in range(2):
                    last = mm(y_ps[:, half, :], diag[:, k % DIAGS, :], v_ring[:, k % ROWS, half * 512:(half + 1) * 512],
                              start and k == 0, False)
                last.then_inc(v_used, 1)

            for key in units.before["y"]:
                wait_done(pe, key)
            for w in range(2 * HEADS):
                if w == HEADS:
                    pe.wait_ge(y_copied, 1)
                for k in range(TOPK):
                    weigh(w, k, w % HEADS == 0)
                    for key in slots.get((w, k), ()):
                        tail_unit(key)
            with pe.Fori(2, TILES) as t:
                pe.wait_ge(y_copied, t)
                for k in range(TOPK):
                    weigh(t * HEADS, k, True)
                with pe.Fori(1, HEADS) as hd:
                    for k in range(TOPK):
                        weigh(t * HEADS + hd, k, False)

        @block.scalar
        def _(sca):
            done = emptied["act"]

            def take(key, dst, src, func=ACT.Copy, **kw):
                wait_full(sca, key)
                nc.scalar.activation(dst, src, func, **kw).then_inc(done, 1)

            for m in range(2):
                for q in range(2):
                    take(("memT", m, q), memT[:, 4 * q:4 * q + 4, m * P:(m + 1) * P], quads(bank(("memT", m, q))))
            for n in range(4):
                take(("kT", n), kT[:, n, :], bank(("kT", n), 0, MEM))
            for c in range(2):
                for m in range(2):
                    take(("vm", c, m), vm[:, m, c * CHUNK:(c + 1) * CHUNK], bank(("vm", c, m), 0, CHUNK))
            take(("bT",), bT[:], bank(("bT",), 0, 50))
            wait_done(sca, ("bT",))
            wait_done(sca, ("beta", 5))
            for r in range(TILES):
                for q in range(2):
                    take(("h0T", r, q), hT[:, 4 * q:4 * q + 4, r * P:(r + 1) * P], quads(bank(("h0T", r, q))))
            for n in range(4):
                take(("z", n), zaT[:, n, :], bank(("z", n)), ACT.Identity, bias=bT[:, n:n + 1])
            for n in list(range(4, 16)) + list(range(22, 26)):
                place = n - 4 if n < 16 else n - 10
                take(("z", n), zT[:, place, :], bank(("z", n)), ACT.Identity, bias=bT[:, n:n + 1])

            def exps(i):
                sca.wait_ge(nm_ready, i + 1)
                if i >= 2:
                    wait_full(sca, ("T1", i - 2))
                key = ("S", i)
                nc.scalar.activation(prob[:, i % 2, 0:768], prob[:, i % 2, 0:768], ACT.Exp, scale=SCALE_B,
                                     bias=nm[:, i % 2, 0:1], accum_out=sums[:, i % 2, 0:1]).then_inc(exp_ready, 1)
                nc.scalar.activation(prob[:, i % 2, 768:1024], two_banks(key, 768, 1024), ACT.Exp, scale=SCALE_C,
                                     bias=nm[:, i % 2, 1:2], accum_out=sums[:, i % 2, 1:2]).then_inc(done, 1)

            exps(0)
            for i in range(PAIRS):
                if i + 1 < PAIRS:
                    exps(i + 1)
                if i >= 2:
                    wait_full(sca, ("O", i - 2))
                take(("T0", i), probT[:, i % 2, 0:4, :], quads(bank(("T0", i))))

            def tail_unit(key):
                what, g = key[0:2]
                if what == "G":
                    j, b = key[2:]
                    at_n = BRANCH_AT[j, b]
                    if at_n >= SIGS or g >= 1:
                        wait_done(sca, ("Yo", g - (at_n < SIGS)) + BRANCH_ORDER[at_n - SIGS])
                    n = 2 * GA[0] + 8 * b + j
                    take(key, sig[:, at_n % SIGS, :], bank(key, 0, GW), ACT.Sigmoid, bias=bT[:, n:n + 1])
                elif what == "h1T":
                    r, q = key[2:]
                    tile = g * GT + r
                    take(key, hT[:, 4 * q:4 * q + 4, tile * P:(tile + 1) * P], quads(bank(key)))
                elif what == "Q":
                    _, tiles, turn, query = query_place(*key[1:])
                    if turn >= 2:
                        wait_full(sca, ("SC",) + query_unit_at(g, turn - 2))
                    elif g >= 1:
                        wait_full(sca, ("SC",) + query_unit_at(g - 1, PARTS[g - 1] * HEADS + turn - 2))
                    take(key, query, bank(key, 0, tiles * P))

            gates, rest = first_tail()
            for key, reader in gates:
                if reader == "act":
                    tail_unit(key)
            for q in range(2):
                tail_unit(("h1T", 0, 0, q))

            def stage_scores(s, slot):
                nc.scalar.copy(s12, step_of(scores, slot)).then_inc(scores_staged, 1)

            def gates_of(s):
                sca.wait_ge(best_ready, s + 1)
                nc.scalar.activation(step_of(gate_all, s), best[:], ACT.Exp, bias=neg_max[:, 0:1],
                                     accum_out=gate_sum[:, bass.ds(s, 1)]).then_inc(gate_ready, 1)

            def activate(s):
                sca.wait_ge(u_used, s * TOPK + TOPK)
                if not first(s):
                    sca.wait_ge(coef_ready, s)
                nc.scalar.activation(act[:], dots[:], ACT.Gelu).then_inc(act_ready, 1)

            def diagonal(s, k):
                if k == 0:
                    sca.wait_ge(coef_ready, s + 1)
                if not first(s):
                    sca.wait_ge(v_used, s * TOPK + (k - TOPK + 1))
                nc.scalar.activation(diag[:, k, :], ident[:], ACT.Copy, scale=coef[:, k:k + 1]).then_inc(diag_ready, 1)

            def copy_y(t):
                sca.wait_ge(v_used, (t + 1) * HEADS * TOPK)
                if t >= 1:
                    sca.wait_ge(out_stored, 16 * t)
                nc.scalar.copy(y_sb, y_ps.rearrange("p a b -> p (a b)")).then_inc(y_copied, 1)

            def window(w, ahead=True, more=True, units_of=None, offset=0):
                for k in range(TOPK):
                    diagonal(w, k)
                    if k == TOPK // 2 and (ahead or more):
                        gates_of(w + 2)
                    if units_of is not None:
                        for key in slots.get((units_of, k), ()):
                            if units.reader[key] == "act":
                                tail_unit(key)
                if ahead:
                    if units_of == 13:
                        wait_done(sca, ("SC", 1, HEADS - 1, 0))
                    stage_scores(w + 3, w + 3 - offset)

            for n in range(HEADS):
                tail_unit(("Q", 0, n, 0))
                if n == 0:
                    wait_done(sca, ("SC", 0, 0, 0))
                    stage_scores(0, 0)
                if n == 3:
                    gates_of(0)
                if n == 5:
                    wait_done(sca, ("SC", 0, 1, 0))
                    stage_scores(1, 1)
            for q in range(2):
                tail_unit(("h1T", 0, 1, q))
            for n in range(HEADS):
                tail_unit(("Q", 0, n, 1))
            gates_of(1)
            activate(0)
            sca.wait_ge(consts, 5)
            wait_done(sca, ("SC", 0, HEADS - 1, 1))
            stage_scores(2, 2)
            for w in range(2 * HEADS):
                if w == HEADS:
                    copy_y(0)
                window(w, units_of=w)
                activate(w + 1)
            copy_y(1)
            with sca.Fori(2 * HEADS, 3 * HEADS - 3) as w:
                window(w)
                activate(w + 1)
            for w in range(3 * HEADS - 3, 3 * HEADS):
                window(w, offset=SCORE_SLOTS)
                activate(w + 1)
            copy_y(2)
            with sca.Fori(3 * HEADS, STEPS - 3) as w:
                window(w, offset=SCORE_SLOTS)
                activate(w + 1)
            window(STEPS - 3, ahead=False)
            activate(STEPS - 2)
            window(STEPS - 2, ahead=False, more=False)
            activate(STEPS - 1)
            window(STEPS - 1, ahead=False, more=False)
            copy_y(3)

        @block.vector
        def _(dve):
            done = emptied["dve"]

            class Chain:

                def __init__(self, base):
                    self.base, self.n = base, 0

                def value(self):
                    return self.base + self.n

                def add(self, *ins):
                    for x in ins:
                        x.then_inc(dve_step, 1)
                        self.n += 1

                def wait(self):
                    dve.wait_ge(dve_step, self.value())
                    if not isinstance(self.base, int):
                        dve.sem_inc(dve_passed)

                def link(self, *ins):
                    self.add(*ins)
                    self.wait()

            c = Chain(0)

            def layer_norm(x, tiles, c, landed, value, ready):
                n = len(tiles)
                at_n = slice(tiles[0], tiles[0] + n)
                for m in range(0, n, GT):
                    for i, r in enumerate(tiles[m:m + GT]):
                        c.add(*[nc.vector.bn_stats(stats[:, i, j, :], x(r)[:, j * 512:(j + 1) * 512])
                                for j in range(2)])
                    c.wait()
                    c.link(*[nc.vector.bn_aggr(moments[:, r, :], stats[:, i, :, :].rearrange("p a b -> p (a b)"))
                             for i, r in enumerate(tiles[m:m + GT])])
                c.link(nc.vector.tensor_scalar(rs[:, 0, at_n], moments[:, at_n, 1], EPS, None, ALU.add))
                c.link(nc.vector.tensor_scalar(rs[:, 1, at_n].bitcast(I32), rs[:, 0, at_n].bitcast(I32), 1, None,
                                               ALU.arith_shift_right))
                c.link(nc.vector.tensor_scalar(rs[:, 2, at_n].bitcast(I32), rs[:, 1, at_n].bitcast(I32), -1.0,
                                               RSQRT_GUESS, ALU.mult, ALU.add))
                for _ in range(3):
                    c.link(nc.vector.tensor_tensor(rs[:, 3, at_n], rs[:, 2, at_n], rs[:, 2, at_n], ALU.mult))
                    c.link(nc.vector.tensor_tensor(rs[:, 3, at_n], rs[:, 3, at_n], rs[:, 0, at_n], ALU.mult))
                    c.link(nc.vector.tensor_scalar(rs[:, 4, at_n], rs[:, 3, at_n], -0.5, 1.5, ALU.mult, ALU.add))
                    c.link(nc.vector.tensor_tensor(rs[:, 2, at_n], rs[:, 2, at_n], rs[:, 4, at_n], ALU.mult))
                dve.wait_ge(landed, value)
                for r in tiles:
                    c.link(nc.vector.scalar_tensor_tensor(
                        out=x(r), in0=x(r), scalar=moments[:, r, 0:1], in1=gains[:, 0, :], op0=ALU.subtract,
                        op1=ALU.mult))
                    nc.vector.scalar_tensor_tensor(
                        out=x(r), in0=x(r), scalar=rs[:, 2, r:r + 1], in1=gains[:, 1, :], op0=ALU.mult,
                        op1=ALU.add).then_inc(ready, 1)

            h_tile = lambda r: h[:, r, :]
            dve.wait_ge(x_in, 16 * TILES)
            layer_norm(h_tile, list(range(TILES)), c, gain_in, 32, h0_ready)
            wait_full(dve, ("KK",))
            dve.wait_ge(consts, 5)
            nc.vector.tensor_copy(KK[0:HD, 0:P], bank(("KK",), 0, P)[0:HD])
            nc.vector.tensor_copy(KK[HD:P, P:2 * P], bank(("KK",), 0, P)[HD:P]).then_inc(done, 1)
            dve.wait_ge(mask_in, 16)
            for b in range(6):
                key = ("beta", b)
                wait_full(dve, key)
                lo, hi = BETA_CUTS[b], BETA_CUTS[b + 1]
                nc.vector.scalar_tensor_tensor(out=beta[:, lo:hi], in0=bank(key, 0, hi - lo)[0:DIL_HEADS],
                                               scalar=1.0 / SCALE_B, in1=mask[:, lo:hi], op0=ALU.mult,
                                               op1=ALU.add).then_inc(done, 1)
            def split(x, high, low):
                c.link(nc.vector.tensor_copy(high, x))
                nc.vector.tensor_tensor(low, x, high.bitcast(F32), ALU.subtract).then_inc(split_ready, 1)

            def split_weights(n):
                _, _, slot, _, value = chunk_at["in", n]
                dve.wait_ge(ring_in[slot], value)
                if QK[2] <= n <= QK[-1]:
                    wait_full(dve, ("z", 2 * (n - 2) + 1))
                high, whole, low = split_chunk(n)
                for i in range(2):
                    rows = slice(4 * i, 4 * i + 4)
                    split(whole[:, rows, :], high[i], low[:, rows, :])

            wait_done(dve, ("h0T", TILES - 1, 1))
            for i in range(2):
                split(hT[:, 4 * i:4 * i + 4, :], hT_high[i], hT_low[:, 4 * i:4 * i + 4, :])
            for r in range(TILES):
                for gg in range(2):
                    key = ("PQ", r, gg)
                    wait_full(dve, key)
                    nc.vector.tensor_copy(pq[:, r, 2 * gg:2 * gg + 2, :], bank(key).rearrange("p (g c) -> p g c", g=2)
                                          ).then_inc(done, 1)
            dve.wait_ge(beta_out, 16)
            half = P // 2
            for g in range(4):
                key = ("Y", g)
                wait_full(dve, key)
                sines = pick[:].rearrange("p x k a -> p (x k a)")[:, (g % 2) * 256:(g % 2) * 256 + ODD]
                c.link(nc.vector.tensor_copy(sines, bank(key, EVEN, EVEN + ODD)))
                tile_of = lambda r: o[r // GT][:, g, (r % GT) * P:(r % GT + 1) * P]
                for at, n, r, to in ((0, P, 1, 0), (P, half, 2, 0), (P + half, half - 1, 0, 1)):
                    even, odd = bank(key, at, at + n), sines[:, at:at + n]
                    nc.vector.tensor_tensor(tile_of(r)[:, to:to + n], even, odd, ALU.add)
                    mirror = tile_of(3 if r == 1 else r)[:, P - n:P]
                    nc.vector.tensor_tensor(mirror[:, ::-1], even, odd, ALU.subtract)
                nc.vector.tensor_copy(tile_of(0)[:, 0:P:half], bank(key, ODD, EVEN)).then_inc(done, 1)
                if g < 2:
                    split_weights(QK[g])
            for n in SPLIT[2:]:
                split_weights(n)
            dve.wait_ge(chan_in, 32)
            def maxima(i):
                key = ("S", i)
                wait_full(dve, key)
                if i >= 2:
                    wait_done(dve, ("S", i - 2))
                    wait_full(dve, ("T1", i - 2))
                r, hd = divmod(i, DIL_HEADS)
                for lo, hi, j, at_mx in ((0, 512, TILES - 1 - r, 0), (512, 768, TABLES - 2, 2)):
                    c.add(nc.vector.tensor_tensor_reduce(
                        prob[:, i % 2, lo:hi], two_banks(key, lo, hi),
                        bias[:, hd, j:j + (hi - lo) // P, :].rearrange("p j m -> p (j m)"), 1.0, LOWEST,
                        ALU.add, ALU.max, mx[:, i % 2, at_mx:at_mx + 1]))
                c.link(nc.vector.tensor_reduce(mx[:, i % 2, 1:2], two_banks(key, 768, 1024), AX.X, ALU.max))
                nc.vector.tensor_scalar(nm[:, i % 2, 0:1], mx[:, i % 2, 0:1], mx[:, i % 2, 2:3], -SCALE_B,
                                        ALU.max, ALU.mult)
                nc.vector.tensor_scalar(nm[:, i % 2, 1:2], mx[:, i % 2, 1:2], -SCALE_C, None, ALU.mult
                                        ).then_inc(nm_ready, 1)

            def normalise(i):
                wait_done(dve, ("S", i))
                dve.wait_ge(exp_ready, i + 1)
                c.link(nc.vector.reciprocal(rinv[:, i % 2, :], sums[:, i % 2, :]))
                nc.vector.tensor_scalar(prob[:, i % 2, 0:768], prob[:, i % 2, 0:768], rinv[:, i % 2, 0:1], None,
                                        ALU.mult)
                nc.vector.tensor_scalar(prob[:, i % 2, 768:1024], prob[:, i % 2, 768:1024], rinv[:, i % 2, 1:2],
                                        None, ALU.mult).then_inc(prob_ready, 1)

            def take_attended(i):
                r, hd = divmod(i, DIL_HEADS)
                key = ("O", i)
                wait_full(dve, key)
                rows = slice(HD * (hd % 2), HD * (hd % 2) + HD)
                cols = slice((r % GT) * P, (r % GT + 1) * P)
                nc.vector.tensor_copy(o[r // GT][rows, 4 + hd // 2, cols], bank(key, 0, P)[rows])
                nc.vector.tensor_copy(o[r // GT][:, 6 + hd, cols], bank(key, P, 2 * P)).then_inc(done, 1)

            dve.wait_ge(beta_out, 16)
            dve.wait_ge(bias_in, 16)
            maxima(0)
            for b in range(3):
                for r in range(TILES):
                    key = ("v", b, r)
                    wait_full(dve, key)
                    nc.vector.tensor_tensor(v_sb[:, r, b * CHUNK:(b + 1) * CHUNK], bank(key, 0, CHUNK),
                                            v_bias[:, b * CHUNK:(b + 1) * CHUNK], ALU.add).then_inc(done, 1)
                if b == 0:
                    normalise(0)
            for i in range(PAIRS + 1):
                if 0 < i < PAIRS:
                    normalise(i)
                if i + 1 < PAIRS:
                    maxima(i + 1)
                if i >= 1:
                    take_attended(i - 1)
                if i < PAIRS:
                    if i >= 2:
                        wait_full(dve, ("O", i - 2))
                    wait_full(dve, ("T1", i))
                    nc.vector.tensor_copy(probT[:, i % 2, 4:8, :], quads(bank(("T1", i)))).then_inc(done, 1)

            def tail_unit(key, c):
                what, g = key[0:2]
                wait_full(dve, key)
                if what == "Yo":
                    j, b = key[2:]
                    wait_done(dve, ("G", g, j, b))
                    n = BRANCH_AT[j, b]
                    if b == 0:
                        nc.vector.tensor_tensor(merged[:, j, :], sig[:, n % SIGS, :], bank(key, 0, GW), ALU.mult
                                                ).then_inc(done, 1)
                    else:
                        c.link(nc.vector.tensor_tensor(part[:, n % 2, :], sig[:, n % SIGS, :], bank(key, 0, GW),
                                                       ALU.mult))
                        wait_done(dve, ("Yo", g, j, b - 1))
                        nc.vector.tensor_tensor(merged[:, j, :], merged[:, j, :], part[:, n % 2, :], ALU.add
                                                ).then_inc(done, 1)
                elif what == "WO":
                    n, r = key[2:]
                    tile = g * GT + r
                    cols = slice(n * CHUNK, (n + 1) * CHUNK)
                    nc.vector.scalar_tensor_tensor(out=h[:, tile, cols], in0=h[:, tile, cols], scalar=ALPHA,
                                                   in1=bank(key, 0, CHUNK), op0=ALU.mult, op1=ALU.add
                                                   ).then_inc(done, 1)
                elif what == "SC":
                    n = key[2]
                    tile, tiles, _, _ = query_place(*key[1:])
                    for r in range(tiles):
                        ins = nc.vector.tensor_copy(scores[:, ((tile + r) * HEADS + n) % SCORE_SLOTS, :],
                                                    bank(key, r * 2 * KEYS, (r + 1) * 2 * KEYS))
                    ins.then_inc(done, 1)

            def first_norm(tiles):
                g, r = divmod(tiles[-1], GT)
                wait_done(dve, ("WO", g, 3, r))
                layer_norm(h_tile, tiles, c, gain_in, 64, h1_ready)

            gates, rest = first_tail()
            for key, reader in gates:
                if reader == "dve":
                    tail_unit(key, c)
            for n in range(4):
                tail_unit(("WO", 0, n, 0), c)
            first_norm([0])
            for n in range(EARLY_WO):
                tail_unit(("WO", 0, n, 1), c)
            def dot(s, k, tile):
                if k == 0 and not first(s):
                    dve.wait_ge(act_ready, s)
                dve.wait_ge(u_landed[k % ROWS], s * 32 + 16 * (k // ROWS) + 16)
                row = u_ring[:, k % ROWS, :]
                nc.vector.tensor_tensor_reduce(row, row, h[:, tile, :], 1.0, 0.0, ALU.mult, ALU.add,
                                               dots[:, k:k + 1]).then_inc(u_used, 1)

            def held(s):
                if not isinstance(s, int):
                    dve.sem_inc(dve_passed)

            def top_halves(s, c):
                dve.wait_ge(scores_staged, s + 1)
                held(s)
                half = lambda t, x: t[:, x * KEYS:(x + 1) * KEYS]
                for r in range(2):
                    lo, hi = 8 * r, 8 * r + 8
                    src = s12 if r == 0 else s12b
                    c.link(*[nc.vector.max(v12[:, x, lo:hi], half(src, x)) for x in range(2)])
                    c.add(*[nc.vector.max_index(i12[:, x, lo:hi], v12[:, x, lo:hi], half(src, x)) for x in range(2)])
                    if r == 0:
                        c.add(*[nc.vector.match_replace(half(s12b, x), v12[:, x, lo:hi], half(src, x), LOWEST)
                                for x in range(2)])
                    c.wait()

            def top_pairs(s, c):
                c.link(nc.vector.tensor_tensor(cand, v12[:, 0, :].unsqueeze(2).broadcast_to([P, TOPK, TOPK]),
                                               v12[:, 1, :].unsqueeze(1).broadcast_to([P, TOPK, TOPK]), ALU.add))
                if not first(s):
                    dve.wait_ge(gate_ready, s)
                    held(s)
                flat = lambda t: t.rearrange("p a b -> p (a b)")
                for r in range(2):
                    lo, hi = 8 * r, 8 * r + 8
                    src = flat(cand if r == 0 else candb)
                    c.link(nc.vector.max(best[:, lo:hi], src))
                    c.add(nc.vector.max_index(pos[:, lo:hi], best[:, lo:hi], src))
                    if r == 0:
                        c.add(nc.vector.match_replace(flat(candb), best[:, lo:hi], src, LOWEST))
                    c.wait()
                nc.vector.tensor_scalar(neg_max[:], best[:, 0:1], -1.0, None, ALU.mult).then_inc(best_ready, 1)
                c.link(nc.vector.tensor_scalar(ab[:, 0, :], pos[:], 4, None, ALU.logical_shift_right),
                       nc.vector.tensor_scalar(ab[:, 1, :], pos[:], TOPK - 1, None, ALU.bitwise_and))
                c.link(nc.vector.tensor_tensor(
                    pick[:].rearrange("p x k a -> p (x k) a"),
                    ab[:].rearrange("p x k -> p (x k)").unsqueeze(2).broadcast_to([P, 2 * TOPK, TOPK]),
                    iota_f[:].unsqueeze(1).broadcast_to([P, 2 * TOPK, TOPK]), ALU.is_equal))
                c.link(nc.vector.tensor_tensor(
                    pick[:], pick[:], i12[:].unsqueeze(2).broadcast_to([P, 2, TOPK, TOPK]), ALU.mult))
                c.link(nc.vector.tensor_reduce(e12[:], pick[:], AX.X, ALU.add))
                nc.vector.scalar_tensor_tensor(out=step_of(expert_all, s), in0=e12[:, 0, :], scalar=float(KEYS),
                                               in1=e12[:, 1, :], op0=ALU.mult, op1=ALU.add).then_inc(expert_ready, 1)

            def coefficients(s, c):
                dve.wait_ge(gate_ready, s + 1)
                c.link(nc.vector.reciprocal(gate_inv[:], gate_sum[:, bass.ds(s, 1)]))
                dve.wait_ge(act_ready, s + 1)
                if not first(s):
                    dve.wait_ge(diag_ready, s * TOPK)
                nc.vector.scalar_tensor_tensor(out=coef[:], in0=step_of(gate_all, s), scalar=gate_inv[:, 0:1],
                                               in1=act[:], op0=ALU.mult, op1=ALU.mult).then_inc(coef_ready, 1)

            def second_norm(t):
                dve.wait_ge(y_copied, t + 1)
                c.link(nc.vector.scalar_tensor_tensor(out=y_sb, in0=h[:, t, :], scalar=ALPHA, in1=y_sb,
                                                      op0=ALU.mult, op1=ALU.add))
                layer_norm(lambda r: y_sb, [t], c, ln2_in, 32, out_ready)

            def window(w, tile, c, ahead=True, units_of=None):
                for k in range(TOPK):
                    dot(w + 1, k, tile)
                    if units_of is not None:
                        for key in slots.get((units_of, k), ()):
                            if units.reader[key] == "dve":
                                tail_unit(key, c)
                if ahead:
                    top_halves(w + 3, c)
                coefficients(w + 1, c)
                if ahead:
                    top_pairs(w + 3, c)

            def windows(lo, hi, tile):
                probe = 22
                with dve.Fori(lo, hi) as w:
                    body = Chain((w - lo) * probe + c.value())
                    window(w, tile, body)
                    assert body.n == probe
                c.n += (hi - lo) * probe

            for n in range(HEADS):
                tail_unit(("SC", 0, n, 0), c)
                if n == 0:
                    top_halves(0, c)
                    top_pairs(0, c)
                    for m in range(EARLY_WO, 4):
                        tail_unit(("WO", 0, m, 1), c)
                if 2 <= n < 6:
                    dot(0, 2 * (n - 2), 0)
                    dot(0, 2 * (n - 2) + 1, 0)
                if n == 3:
                    first_norm([1])
            top_halves(1, c)
            top_pairs(1, c)
            for n in range(HEADS):
                dot(0, ROWS + n, 0)
                tail_unit(("SC", 0, n, 1), c)
            coefficients(0, c)
            top_halves(2, c)
            top_pairs(2, c)
            for w in range(2 * HEADS):
                if w == 10:
                    first_norm([2, 3])
                if w == 14:
                    second_norm(0)
                window(w, (w + 1) // HEADS, c, units_of=w)
            for t in (2, 3):
                lo = t * HEADS
                windows(lo, lo + 2, t)
                second_norm(t - 1)
                if t == 2:
                    windows(lo + 2, lo + HEADS - 1, t)
                    window(lo + HEADS - 1, t + 1, c)
                else:
                    windows(lo + 2, STEPS - 3, t)
            for w in (STEPS - 3, STEPS - 2):
                window(w, TILES - 1, c, ahead=False)
            second_norm(TILES - 1)


def t5_bucket(rel):
    half, exact = BUCKETS // 2, BUCKETS // 4
    n = np.abs(rel)
    nf = np.maximum(n, 1).astype(np.float32)
    large = exact + (np.log(nf / exact) / np.float32(math.log(1024 / exact)) * (half - exact)).astype(np.int32)
    return np.where(rel > 0, half, 0) + np.where(n < exact, n, np.minimum(large, half - 1))


def shape_constants():
    step = np.arange(DELTAS) - (P - 1)
    onehot = np.zeros((BUCKETS, TABLES, DELTAS), np.float32)
    mask = np.zeros((DIL_HEADS, TABLES, DELTAS), np.float32)
    for j in range(TABLES):
        rel = TILES * step
        if j < TABLES - 2:
            rel = rel + (j - (TILES - 1))
            allowed = np.abs(rel) <= 64
        elif j == TABLES - 2:
            allowed = np.abs(step) <= 64
        else:
            allowed = step % 4 == 0
        onehot[t5_bucket(rel), j, np.arange(DELTAS)] = 1.0
        mask[:, j, ~allowed] = -1e30
    by_tile = np.arange(SEQ).reshape(P, TILES).T
    token = by_tile.reshape(-1)
    freq = np.concatenate([by_tile[1], by_tile[2, :P // 2], by_tile[0, 1:P // 2], by_tile[0, [0, P // 2]]])
    angle = 2 * math.pi / SEQ * ((token[:, None] * freq[None, :]) % SEQ)
    ch = np.arange(P)
    phi = 2 * math.pi / P * ((ch[:, None] * ch[None, :]) % P)
    norm = 1.0 / math.sqrt(SEQ * P)
    return {
        "c_onehot": onehot.reshape(BUCKETS, -1),
        "c_mask": mask.reshape(DIL_HEADS, -1),
        "c_chan": (np.concatenate([np.cos(phi), np.sin(phi)], 1) * norm).astype(np.float32),
        "c_cos": np.cos(angle).astype(np.float32),
        "c_sin": (-np.sin(angle[:, :ODD])).astype(np.float32),
    }


_INS = ["x", "mem", "rel_bias", "ln0_g", "ln0_b", "w_in", "b_in", "w_a", "w_b", "w_c", "w_mem_kv", "w_o",
        "ln1_g", "ln1_b", "w_pq", "sub_keys1", "sub_keys2", "u_tab", "v_tab", "ln2_g", "ln2_b"]


def kernel(**inputs):
    import numpy as _np
    import concourse.bacc as _bacc
    from concourse import mybir as _mybir
    from concourse.bass_utils import run_bass_kernel_spmd as _run

    nc = _bacc.Bacc("TRN2", target_bir_lowering=False, num_devices=1)
    arrays, args = {}, {}
    given = {name: _np.ascontiguousarray(inputs[name]) for name in _INS}
    for name, a in {**given, **shape_constants()}.items():
        arrays[f"in_{name}_dram"] = a
        args[name] = nc.dram_tensor(f"in_{name}_dram", a.shape, _mybir.dt.from_np(a.dtype), kind="ExternalInput").ap()
    args["out"] = nc.dram_tensor("out_0_dram", (1, SEQ, D), F32, kind="ExternalOutput").ap()
    build(nc, **args)
    r = _run(nc, [arrays], core_ids=[0])
    return r.results[0]["out_0_dram"]
```
